# Optimizing a Trainium2 kernel written in Bass

```python
import functools
import jax, jax.numpy as jnp
from jax import lax
import numpy as np

D_MODEL = 1024
BATCH = 1
SEQ = 128
DEPTH = 1
DEC_BATCH = 1
DEC_SEQ = 256
PAST_LEN = 128

GRID_W = 64
H_A = 8
DH_A = 64
D_A = H_A * DH_A
WIN_H_MAX = 8
WIN_W = 16
KEY_BLOCK_W = 2 * WIN_W
D_CONV = 512
CONV_W = 3
H_C = 4
DK_C = 128
DV_C = 128
D_CK = H_C * DK_C
D_CV = H_C * DV_C
CHUNK = 16
N_EXPERTS = 64
N_GROUPS = 8
EXPERTS_PER_GROUP = N_EXPERTS // N_GROUPS
TOPK_GROUPS = 4
TOP_K = 8
D_EXPERT = 256
D_SHARED = 256
ROUTED_SCALE = 2.5
N_MOD = 6
EPS = 1e-6
NEG_BIG = -1e30
LOG_FLOOR = 1e-30
SPLIT_SIZES = (D_A, D_A, D_A, D_CONV, D_CONV, D_CONV, D_CK, D_CK, D_CK, D_CV, D_CV, D_MODEL, D_MODEL, D_MODEL)
D_IN = 3 * D_A + 3 * D_CONV + 3 * D_CK + 2 * D_CV + 3 * D_MODEL

kernel_name = 'hybrid_diffusion_na_conv_hgrn2_moe_step'

def rmsnorm(x, g):
    xf = x.astype(jnp.float32)
    y = xf * lax.rsqrt(jnp.mean(xf * xf, axis=-1, keepdims=True) + EPS)
    return (y * g.astype(jnp.float32)).astype(x.dtype)

def lower_bounds(p):
    sm = jax.nn.softmax(p.astype(jnp.float32), axis=0)
    return jnp.cumsum(sm, axis=0) - sm[0:1]

def ctx_attention(q, k, v):
    bsz, t, h, dh = q.shape
    s = jnp.einsum('bqhd,bkhd->bhqk', q, k).astype(jnp.float32) * (dh ** -0.5)
    p = jax.nn.softmax(s, axis=-1).astype(v.dtype)
    return jnp.einsum('bhqk,bkhd->bqhd', p, v).reshape(bsz, t, h * dh)

def na_latent(q, k, v, ck, cv, rpb_l):
    bsz, t, h, dh = q.shape
    rows = t // GRID_W
    kh = min(WIN_H_MAX, rows)
    nbw = GRID_W // WIN_W
    r = np.arange(rows)
    row_idx = np.clip(r - kh // 2, 0, rows - kh)[:, None] + np.arange(kh)[None, :]
    cols = np.arange(GRID_W)
    col_start = np.clip(cols - WIN_W // 2, 0, GRID_W - WIN_W)
    blk_start = np.minimum(col_start[::WIN_W], GRID_W - KEY_BLOCK_W)
    col_idx = blk_start[:, None] + np.arange(KEY_BLOCK_W)[None, :]
    q_cols = cols.reshape(nbw, WIN_W)
    q_start = col_start.reshape(nbw, WIN_W)
    kc = col_idx[:, None, :]
    valid = (kc >= q_start[:, :, None]) & (kc < q_start[:, :, None] + WIN_W)
    dc_idx = np.clip(kc - q_cols[:, :, None] + WIN_W - 1, 0, 2 * WIN_W - 2)
    dr_idx = row_idx - r[:, None] + WIN_H_MAX - 1
    bias = rpb_l[:, dr_idx[:, None, None, :, None], dc_idx[None, :, :, None, :]]
    bias = jnp.where(valid[None, None, :, :, None, :], bias.astype(jnp.float32), NEG_BIG)
    bias = bias.transpose(1, 2, 0, 3, 4, 5).reshape(rows, nbw, h, WIN_W, kh * KEY_BLOCK_W)
    ri = row_idx[:, None, :, None]
    ci = col_idx[None, :, None, :]
    kg = k.reshape(bsz, rows, GRID_W, h, dh)
    vg = v.reshape(bsz, rows, GRID_W, h, dh)
    n_lat = kh * KEY_BLOCK_W
    k_blk = kg[:, ri, ci].reshape(bsz, rows, nbw, n_lat, h, dh)
    v_blk = vg[:, ri, ci].reshape(bsz, rows, nbw, n_lat, h, dh)
    qb = q.reshape(bsz, rows, nbw, WIN_W, h, dh)
    scale = dh ** -0.5
    s_lat = jnp.einsum('brjqhd,brjnhd->brjhqn', qb, k_blk).astype(jnp.float32) * scale + bias
    s_ctx = jnp.einsum('brjqhd,bchd->brjhqc', qb, ck).astype(jnp.float32) * scale
    p = jax.nn.softmax(jnp.concatenate([s_lat, s_ctx], axis=-1), axis=-1).astype(v.dtype)
    o = (jnp.einsum('brjhqn,brjnhd->brjqhd', p[..., :n_lat], v_blk)
         + jnp.einsum('brjhqc,bchd->brjqhd', p[..., n_lat:], cv))
    return o.reshape(bsz, t, h * dh)

def conv_branch(u, gb, gc, w):
    z = gc * u
    zp = jnp.pad(z, ((0, 0), (1, 1), (0, 0)))
    y = w[0] * zp[:, :-2] + w[1] * zp[:, 1:-1] + w[2] * zp[:, 2:]
    return gb * y

def gla_chunk(q, k, v, logf, s0):
    bsz, t, h, dk = q.shape
    dv = v.shape[-1]
    n = t // CHUNK

    def blk(a):
        return a.reshape(bsz, n, CHUNK, h, a.shape[-1]).transpose(0, 3, 1, 2, 4)

    q, k, v, logf = blk(q), blk(k), blk(v), blk(logf)
    b = jnp.cumsum(logf, axis=3)
    causal = np.tril(np.ones((CHUNK, CHUNK), dtype=bool))
    diff = b[:, :, :, :, None, :] - b[:, :, :, None, :, :]
    decay = jnp.exp(jnp.where(causal[:, :, None], diff, NEG_BIG))
    attn = jnp.einsum('bhntd,bhnsd,bhntsd->bhnts', q, k, decay)
    o_intra = jnp.einsum('bhnts,bhnsv->bhntv', attn, v)
    b_last = b[:, :, :, -1:, :]
    kv = jnp.einsum('bhnsd,bhnsv->bhndv', k * jnp.exp(b_last - b), v)
    chunk_decay = jnp.exp(b_last[:, :, :, 0, :])

    def step(s, inp):
        dec, kv_n = inp
        return dec[..., None] * s + kv_n, s

    s_final, s_prev = lax.scan(step, s0, (jnp.moveaxis(chunk_decay, 2, 0), jnp.moveaxis(kv, 2, 0)))
    o_inter = jnp.einsum('bhntd,nbhdv->bhntv', q * jnp.exp(b), s_prev)
    o = (o_intra + o_inter).transpose(0, 2, 3, 1, 4).reshape(bsz, t, h, dv)
    return o, s_final

def hgrn_branch(q, zf, zb, i, og, lb_f, lb_b, norm_g, s0f, s0b):
    bsz, t, _ = q.shape
    f32 = jnp.float32
    qh = q.astype(f32).reshape(bsz, t, H_C, DK_C)
    vh = i.astype(f32).reshape(bsz, t, H_C, DV_C)

    def gates(z, lb):
        z = z.astype(f32).reshape(bsz, t, H_C, DK_C)
        lb = lb.reshape(H_C, DK_C)
        logf = jnp.logaddexp(jnp.log1p(-lb) + jax.nn.log_sigmoid(z), jnp.log(jnp.maximum(lb, LOG_FLOOR)))
        key = (1.0 - lb) * jax.nn.sigmoid(-z)
        return logf, key

    lf_f, k_f = gates(zf, lb_f)
    lf_b, k_b = gates(zb, lb_b)
    o_f, s_f = gla_chunk(qh, k_f, vh, lf_f, s0f)
    rev = lambda a: jnp.flip(a, axis=1)
    o_b, s_b = gla_chunk(rev(qh), rev(k_b), rev(vh), rev(lf_b), s0b)
    o = o_f + rev(o_b)
    o = o * lax.rsqrt(jnp.mean(o * o, axis=-1, keepdims=True) + EPS) * norm_g.astype(f32).reshape(H_C, DV_C)
    o = o.reshape(bsz, t, D_CV) * jax.nn.silu(og.astype(f32))
    return o.astype(q.dtype), s_f, s_b

def moe(x, lp):
    n_tok = x.shape[0]
    s = jax.nn.sigmoid((x @ lp['w_router']).astype(jnp.float32))
    sel = s + lp['b_router'].astype(jnp.float32)
    grp_score = lax.top_k(sel.reshape(n_tok, N_GROUPS, EXPERTS_PER_GROUP), 2)[0].sum(-1)
    _, gidx = lax.top_k(grp_score, TOPK_GROUPS)
    gmask = jax.nn.one_hot(gidx, N_GROUPS, dtype=jnp.float32).sum(-2) > 0
    emask = jnp.repeat(gmask, EXPERTS_PER_GROUP, axis=-1)
    _, eidx = lax.top_k(jnp.where(emask, sel, NEG_BIG), TOP_K)
    w = jnp.take_along_axis(s, eidx, axis=-1)
    w = w / jnp.sum(w, axis=-1, keepdims=True) * ROUTED_SCALE
    combine = jnp.einsum('nk,nke->ne', w, jax.nn.one_hot(eidx, N_EXPERTS, dtype=jnp.float32)).astype(x.dtype)
    hg = jnp.einsum('nd,edf->nef', x, lp['w_gate'])
    hu = jnp.einsum('nd,edf->nef', x, lp['w_up'])
    hid = jax.nn.silu(hg) * hu * combine[:, :, None]
    y = jnp.einsum('nef,efd->nd', hid, lp['w_down'])
    sh = (jax.nn.silu(x @ lp['w_sh_gate']) * (x @ lp['w_sh_up'])) @ lp['w_sh_down']
    return y + sh

def trunk_layer(h, ada, lp, attend, s0f, s0b):
    bsz, t, _ = h.shape
    sh1, sc1, g1, sh2, sc2, g2 = jnp.split(ada, N_MOD, axis=-1)
    n = rmsnorm(h, lp['norm1_g']) * (1 + sc1) + sh1
    split_idx = np.cumsum(SPLIT_SIZES)[:-1].tolist()
    (qa, ka, va, u, gb, gc, qc, zf, zb, ic, oc, ga, gbr, gcr) = jnp.split(n @ lp['w_in'], split_idx, axis=-1)
    heads = lambda a: a.reshape(bsz, t, H_A, DH_A)
    ka, va = heads(ka), heads(va)
    o_a = attend(heads(qa), ka, va)
    o_b = conv_branch(u, gb, gc, lp['w_conv'])
    o_c, s_f, s_b = hgrn_branch(qc, zf, zb, ic, oc, lp['lb_f'], lp['lb_b'], lp['hgrn_g'], s0f, s0b)
    mix = (jax.nn.sigmoid(ga) * (o_a @ lp['w_br_a'])
           + jax.nn.sigmoid(gbr) * (o_b @ lp['w_br_b'])
           + jax.nn.sigmoid(gcr) * (o_c @ lp['w_br_c'])) @ lp['w_out']
    h = h + g1 * mix
    n2 = rmsnorm(h, lp['norm2_g']) * (1 + sc2) + sh2
    y = moe(n2.reshape(bsz * t, D_MODEL), lp).reshape(bsz, t, D_MODEL)
    h = h + g2 * y
    return h, ka, va, s_f, s_b

def setup_inputs(seed: int = 0) -> dict:
    key = jax.random.key(seed)
    ks = jax.random.split(key, 32)
    f32 = jnp.float32
    nrm = lambda kk, shape, sc: jax.random.normal(kk, shape, f32) * sc
    D = D_MODEL
    return {
        'x_prompt': nrm(ks[0], (BATCH, SEQ, D), 1.0),
        'x_sample': nrm(ks[1], (DEC_BATCH, DEC_SEQ, D), 1.0),
        'cache_k': nrm(ks[2], (DEC_BATCH, DEPTH, PAST_LEN, H_A, DH_A), 1.0),
        'cache_v': nrm(ks[3], (DEC_BATCH, DEPTH, PAST_LEN, H_A, DH_A), 1.0),
        'state_hgrn': nrm(ks[4], (DEC_BATCH, DEPTH, 2, H_C, DK_C, DV_C), 0.5),
        'c': nrm(ks[5], (DEC_BATCH, D), 1.0),
        'c_ctx': nrm(ks[6], (D,), 1.0),
        'norm1_g': 1.0 + nrm(ks[7], (DEPTH, D), 0.01),
        'norm2_g': 1.0 + nrm(ks[8], (DEPTH, D), 0.01),
        'w_ada': nrm(ks[9], (DEPTH, D, N_MOD * D), 0.3 * D ** -0.5),
        'b_ada': nrm(ks[10], (DEPTH, N_MOD * D), 0.01),
        'w_in': nrm(ks[11], (DEPTH, D, D_IN), D ** -0.5),
        'rpb': nrm(ks[12], (DEPTH, H_A, 2 * WIN_H_MAX - 1, 2 * WIN_W - 1), 0.1),
        'w_conv': nrm(ks[13], (DEPTH, CONV_W, D_CONV), CONV_W ** -0.5),
        'lb_fwd': nrm(ks[14], (DEPTH, D_CK), 0.1),
        'lb_bwd': nrm(ks[15], (DEPTH, D_CK), 0.1),
        'hgrn_norm_g': 1.0 + nrm(ks[16], (DEPTH, D_CV), 0.01),
        'w_br_a': nrm(ks[17], (DEPTH, D_A, D), D_A ** -0.5),
        'w_br_b': nrm(ks[18], (DEPTH, D_CONV, D), D_CONV ** -0.5),
        'w_br_c': nrm(ks[19], (DEPTH, D_CV, D), D_CV ** -0.5),
        'w_out': nrm(ks[20], (DEPTH, D, D), D ** -0.5),
        'w_router': nrm(ks[21], (DEPTH, D, N_EXPERTS), D ** -0.5),
        'b_router': nrm(ks[22], (DEPTH, N_EXPERTS), 0.01),
        'w_gate': nrm(ks[23], (DEPTH, N_EXPERTS, D, D_EXPERT), D ** -0.5),
        'w_up': nrm(ks[24], (DEPTH, N_EXPERTS, D, D_EXPERT), D ** -0.5),
        'w_down': nrm(ks[25], (DEPTH, N_EXPERTS, D_EXPERT, D), D_EXPERT ** -0.5),
        'w_sh_gate': nrm(ks[26], (DEPTH, D, D_SHARED), D ** -0.5),
        'w_sh_up': nrm(ks[27], (DEPTH, D, D_SHARED), D ** -0.5),
        'w_sh_down': nrm(ks[28], (DEPTH, D_SHARED, D), D_SHARED ** -0.5),
        'final_norm_g': 1.0 + nrm(ks[29], (D,), 0.01),
    }

def reference(x_prompt, x_sample, cache_k, cache_v, state_hgrn, c, c_ctx, norm1_g, norm2_g, w_ada, b_ada,
              w_in, rpb, w_conv, lb_fwd, lb_bwd, hgrn_norm_g, w_br_a, w_br_b, w_br_c, w_out, w_router,
              b_router, w_gate, w_up, w_down, w_sh_gate, w_sh_up, w_sh_down, final_norm_g):
    f32 = jnp.float32
    lbs_f = lower_bounds(lb_fwd)
    lbs_b = lower_bounds(lb_bwd)

    def layer_params(l):
        return {'norm1_g': norm1_g[l], 'norm2_g': norm2_g[l], 'w_in': w_in[l], 'w_conv': w_conv[l],
                'lb_f': lbs_f[l], 'lb_b': lbs_b[l], 'hgrn_g': hgrn_norm_g[l],
                'w_br_a': w_br_a[l], 'w_br_b': w_br_b[l], 'w_br_c': w_br_c[l], 'w_out': w_out[l],
                'w_router': w_router[l], 'b_router': b_router[l], 'w_gate': w_gate[l], 'w_up': w_up[l],
                'w_down': w_down[l], 'w_sh_gate': w_sh_gate[l], 'w_sh_up': w_sh_up[l], 'w_sh_down': w_sh_down[l]}

    h = x_prompt
    zero_state = jnp.zeros((x_prompt.shape[0], H_C, DK_C, DV_C), f32)
    ks_list, vs_list, st_list = [], [], []
    for l in range(DEPTH):
        ada = jax.nn.silu(c_ctx) @ w_ada[l] + b_ada[l]
        h, k_l, v_l, s_f, s_b = trunk_layer(h, ada, layer_params(l), ctx_attention, zero_state, zero_state)
        ks_list.append(k_l)
        vs_list.append(v_l)
        st_list.append(jnp.stack([s_f, s_b], axis=1))
    y_prompt = rmsnorm(h, final_norm_g)
    new_cache_k = jnp.stack(ks_list, axis=1)
    new_cache_v = jnp.stack(vs_list, axis=1)
    new_state_hgrn = jnp.stack(st_list, axis=1)

    g = x_sample
    for l in range(DEPTH):
        ada = (jax.nn.silu(c) @ w_ada[l] + b_ada[l])[:, None, :]
        attend = functools.partial(na_latent, ck=cache_k[:, l], cv=cache_v[:, l], rpb_l=rpb[l])
        g, _, _, _, _ = trunk_layer(g, ada, layer_params(l), attend,
                                    state_hgrn[:, l, 0].astype(f32), state_hgrn[:, l, 1].astype(f32))
    y_sample = rmsnorm(g, final_norm_g)
    return (y_prompt, y_sample, new_cache_k, new_cache_v, new_state_hgrn)


_drawn_inputs = setup_inputs


def setup_inputs(seed=0):
    import zlib

    import numpy as np

    out = dict(_drawn_inputs(seed))
    spreads = {}
    factors = {'cache_k': 3.963,
     'cache_v': 10.663,
     'state_hgrn': 30.156,
     'norm1_g': 5.281,
     'norm2_g': 14.317,
     'b_ada': 2.895,
     'rpb': 49.465,
     'hgrn_norm_g': 39.192,
     'final_norm_g': 34.444}
    for name, (base, spread) in spreads.items():
        noise = np.random.default_rng([zlib.crc32(name.encode()), seed]).standard_normal(out[name].shape)
        drawn = base * np.exp(spread * noise) if base else spread * noise
        out[name] = __import__('jax').numpy.asarray(drawn.astype(out[name].dtype))
    for name, factor in factors.items():
        out[name] = (out[name] * factor).astype(out[name].dtype)
    return out
```

```python
from contextlib import ExitStack

import numpy as np

import concourse.bass as bass
from concourse import mybir

F32 = mybir.dt.float32
I32 = mybir.dt.int32
U32 = mybir.dt.uint32
ALU = mybir.AluOpType
ACT = mybir.ActivationFunctionType
AX = mybir.AxisListType

P = 128
D = 1024
KD = D // P
NT = 3
T = NT * P
CTX = P
GRID_W = 64
NH, DH = 8, 64
HC = 4
WCH = 512
NE, TOPK, NG, TOPG = 64, 8, 8, 4
DE = 256
ROUTED_SCALE = 2.5
EPS = 1e-6
NEG_BIG = -1e30
LOG_FLOOR = 1e-30
LEVELS = (2, 4, 8, 16, 32, 64, 128)
ROUNDS = NE + (T * TOPK - NE) // P
RTAB = P
BODY = 12
PASSES = (ROUNDS + BODY - 1) // BODY
WS, XGS, AHEAD = 3, 4, 4

K_ID, K_MASK, K_LEV, K_SCAN, K_SEL, K_TRI, K_ONE, K_R128, K_TOK, K_COL, K_T8, K_END = range(12)
K_W = [P, GRID_W, 7 * P, T, 2 * P, P, P, P, NT * 3, 2, NG * NG, 0]
K_AT = [sum(K_W[:i]) for i in range(12)]
C_N1, C_N2, C_C, C_ADA, C_LB, C_CONV, C_HG = range(7)
C_W = [KD, KD, 2 * KD, 4 * KD, 2 * HC, 12, HC]
C_AT = [sum(C_W[:i]) for i in range(8)]


def shape_constants():
    k = np.zeros((P, K_AT[K_END]), np.float32)
    p = np.arange(P)
    put = lambda i, a: k.__setitem__((slice(None), slice(K_AT[i], K_AT[i] + K_W[i])), a)
    put(K_ID, np.eye(P))
    qc = (GRID_W - 1 - p % GRID_W)[:, None]
    kc = np.arange(GRID_W)[None, :]
    start = np.clip(qc - 8, 0, GRID_W - 16)
    put(K_MASK, np.where((kc >= start) & (kc < start + 16), 0.0, NEG_BIG))
    s, t = p[:, None], p[None, :]
    put(K_LEV, np.concatenate([((s // L == t // L) & ((s % L < L // 2) != (t % L < L // 2))) for L in LEVELS], 1))
    put(K_SCAN, np.tile((np.arange(T) % P != 0).astype(np.float32), (P, 1)))
    sel = np.zeros((P, 2, P)); sel[0, 0] = 1; sel[1, 1] = 1
    put(K_SEL, sel.reshape(P, -1))
    put(K_TRI, (s < t))
    put(K_ONE, np.ones((P, P)))
    put(K_R128, np.tile(p[None, :].astype(np.float32), (P, 1)))
    tok = np.stack([np.stack([p + P * m, np.ones(P), np.zeros(P)], 1) for m in range(NT)], 1)
    put(K_TOK, tok.reshape(P, -1))
    put(K_COL, np.stack([p, p + T], 1))
    g = np.arange(NG)
    put(K_T8, np.tile((g[None, :] < g[:, None]).astype(np.float32).reshape(1, -1), (P, 1)))
    return k


STREAM = ([("ada", n) for n in range(4)]
          + [("in", n) for n in range(17)]
          + [("ada", n) for n in range(4, 12)]
          + [("br", n) for n in range(3)]
          + [("out", n) for n in range(2)]
          + [("sh", 0), ("shd", 0)])
SLOT_OF = {key: n for n, key in enumerate(STREAM)}
NSLOT = 3
IN_CHUNKS = ["q", "k", "v", "u", "gb", "gc", "qc", "zf", "zb", "ic", "oc"] + [f"g{n}" for n in range(6)]
TOK_CHUNKS = ("v", "ic")


def projection_units():
    units = []
    for n in range(4):
        units.append(("ada", n, 0))
    for c, name in enumerate(IN_CHUNKS):
        for j in range(NT if name in TOK_CHUNKS else 4):
            units.append((name, c, j))
    for n in range(4, 12):
        units.append(("ada", n, 0))
    return units


UNITS = projection_units()
AFTER = {}
for _n, (_name, _c, _j) in enumerate(UNITS):
    AFTER[("ada", _c) if _name == "ada" else _name] = _n + 1


def schedule():
    s = [("norm1",)]
    att = 0
    fill = []
    for n, (name, c, j) in enumerate(UNITS):
        if n + 1 > AFTER["zb"]:
            fill.append(("unit", n))
            continue
        s.append(("unit", n))
        if n + 1 == AFTER[("ada", 3)]:
            s.append(("mod1",))
        if n + 1 > AFTER["v"] and att <= NH:
            if att > 0:
                s.append(("values", att - 1))
            if att < NH:
                s.append(("scores", att))
            att += 1
        if n + 1 == AFTER["gc"]:
            s.append(("conv",))
        if n + 1 == AFTER["v"]:
            s.append(("cache",))
    stages = [(("gates",), 2), (("decays",), 3), (("ops", 0), 1)]
    for i in range(16):
        stages += [(("level", i), 0), (("ops", i + 1) if i < 15 else ("carry",), 1 if i < 15 else 2)]
    stages += [(("carry_t",), 2), (("carry_products",), 2), (("hout", 0), 1), (("hout_t", 0), 1), (("hout", 1), 1),
               (("hout_t", 1), 1), (("hout", 2), 1), (("hout_t", 2), 0)]
    for stage, n in stages:
        s += [stage] + fill[:n]
        fill = fill[n:]
    late = [("late_act", b) for b in range(3)]
    while fill or late:
        s += late[:1] + fill[:1]
        late, fill = late[1:], fill[1:]
    s += [("mod2",), ("branches",), ("wout",), ("norm2",), ("router",)]
    s += [("shared", m) for m in range(NT)] + [("table",)]
    return s


SCHEDULE = schedule()
assert [x for x in SCHEDULE if x[0] == "values"][-1][1] == NH - 1


def trunk(nc, x, consts, cols, b_gate, w_ada, w_in, w_br, w_out, rpb, cache_k, cache_v, state, w_router, b_router,
          w_sh_gate, w_sh_up, w_sh_down, w_gate, w_up, w_down, final_g, y, new_k, new_v, new_state):
    n2_rows = nc.dram_tensor("n2_rows", (4 * P, D), F32, kind="Internal").ap()
    y_rows = nc.dram_tensor("y_rows", (4 * P, D), F32, kind="Internal").ap()
    with ExitStack() as ctx:
        def sb(name, shape, dt=F32):
            return ctx.enter_context(nc.sbuf_tensor(name, shape, dt))

        def sem(name):
            return ctx.enter_context(nc.semaphore(name))

        PS = ctx.enter_context(nc.psum_tensor("PS", [P, 8, 512], F32))

        K = sb("K", [P, K_AT[K_END]])
        C = sb("C", [P, C_AT[7]])
        kc = lambda i: K[:, K_AT[i]:K_AT[i] + K_W[i]]
        cc = lambda i: C[:, C_AT[i]:C_AT[i] + C_W[i]]
        ident = kc(K_ID)
        levmask = kc(K_LEV).bitcast(U32).rearrange("p (l t) -> p l t", l=7)
        sel = kc(K_SEL).rearrange("p (v t) -> p v t", v=2)
        ones = kc(K_ONE)
        nT = sb("nT", [P, KD, T])
        small = sb("small", [P, 128])
        modc = sb("modc", [P, 4, 2, KD])
        csil = sb("csil", [P, KD, 2])
        bigA = sb("bigA", [P, NSLOT * 4096])
        bigB = sb("bigB", [P, 24608])
        bigC = sb("bigC", [P, 5760])
        bigD = sb("bigD", [P, 3 * 1536])
        ring = bigA[:, :].rearrange("p (s n) -> p s n", s=NSLOT)

        def cut(t, at, shape, names="abcd"):
            n = int(np.prod(shape))
            v = t[:, at:at + n]
            if len(shape) == 1:
                return v
            ax = names[:len(shape)]
            return v.rearrange("p (" + " ".join(ax) + ") -> p " + " ".join(ax), **dict(zip(ax[:-1], shape[:-1])))

        G = cut(bigB, 0, (24, T))
        X = cut(bigB, 0, (NT, D))
        XN = cut(bigB, 3072, (NT, D))
        ADA = bigB[:, 6144:8192]
        CK = bigB[:, 8192:8704]
        CKO = bigB[:, 8704:9216]
        ATT = 9216
        Q = cut(bigB, ATT, (4, T))
        KT = cut(bigB, ATT + 1536, (4, T))
        V = cut(bigB, ATT + 3072, (NT, 512))
        E = cut(bigB, ATT, (2, 768))
        QX = bigB[:, ATT + 1536:ATT + 2304]
        KX = bigB[:, ATT + 2304:ATT + 3072]
        KH = cut(bigB, ATT, (4, HC, P))
        KHT = cut(bigB, ATT + 2048, (4, HC, P))
        ST2 = cut(bigB, ATT, (2, HC, P))
        XH = cut(bigB, ATT, (NT, D))
        T1 = bigB[:, ATT + 3072:ATT + 3584]
        FG = bigB[:, ATT + 3584:ATT + 4608]
        UU = cut(bigB, 13824, (4, T))
        AT_ = cut(bigB, 13824, (HC, NT, P))
        OCT = UU
        GB = cut(bigB, 15360, (4, T))
        GC = cut(bigB, 16896, (4, 388))
        ZP = cut(bigB, 18448, (4, 388))
        KEY = cut(bigB, 16896, (2, HC, T))
        BG = bigB[:, 16896:18944]
        QC = cut(bigB, 20000, (HC, T))
        Z = cut(bigB, 21536, (2, HC, T))
        GR = bigB[:, 20000:22048]
        Zrows = bigB[0:2, 22048:24096]
        BIAS = cut(bigC, 0, (2, 2, T))
        CV = bigC[:, 1536:2048]
        CKT = cut(bigC, 2048, (4, P))
        SB = cut(bigC, 2560, (3, T))
        PR = cut(bigC, 3712, (3, T))
        PT = cut(bigC, 4864, (3, 2 * P))
        PTC = bigC[:, 5632:5760]
        EB = cut(bigC, 0, (2, HC, 2 * P))
        STC = cut(bigC, 2048, (2, HC, P))
        OS, OQ, OR = bigC[:, 3072:3584], bigC[:, 3584:4096], bigC[:, 4096:4608]
        ST = cut(bigC, 4608, (2, HC, P))
        GBC = cut(bigC, 0, (2, 2, D))
        IC = cut(bigD, 0, (NT, 512))
        OG = cut(bigD, 1536, (HC, T))
        OA = cut(bigD, 3072, (4, T))
        WSLOT = [bigB[:, 0:6144], bigA[:, 0:6144], bigA[:, 6144:12288]]
        GU_W = [w[:, 0:4096].rearrange("p (k n) -> p k n", k=KD) for w in WSLOT]
        DN_W = [w[:, 4096:6144].rearrange("p (k n) -> p k n", k=2) for w in WSLOT]
        XN2 = cut(bigB, 0, (NT, D))
        N2 = cut(bigB, 3072, (NT, D))
        XG = cut(bigB, 16896, (XGS, D))
        HID = cut(bigB, 8192, (2, DE))
        HT = cut(bigB, 8704, (2, 2, P))
        SHO = cut(bigB, 13824, (NT, D))
        XT = cut(bigB, 6144, (2, KD, P))
        YS = cut(bigB, 22016, (2, D))
        HS = cut(bigB, 24064, (2, DE))
        WR = cut(bigD, 0, (KD, NE))
        BR = bigD[:, 512:576]
        SG = cut(bigD, 576, (NT, NE))
        SE = cut(bigD, 768, (NT, NE))
        SM = cut(bigD, 960, (NT, NE))
        MK = cut(bigD, 1152, (NT, NE))
        WW = cut(bigD, 1344, (NT, NE))
        M8 = cut(bigD, 1536, (NT, NG, 8))
        CMP = cut(bigD, 1728, (NT, NG, NG))
        CM2 = cut(bigD, 1920, (NT, NG, NG))
        CNT, NEX, END, STA, EON, TMP = (bigD[:, 2112 + 64 * i:2176 + 64 * i] for i in range(6))
        TE = cut(bigD, 2496, (7, P))
        POSR = cut(bigD, 3392, (NT, P))
        COMB = cut(bigD, 3776, (NT, P))
        GS = cut(bigD, 4160, (NT, NG))
        GK = cut(bigD, 4184, (NT, NG))
        T8 = cut(bigD, 4208, (NT, 8))
        WSUM = bigD[:, 4232:4235]
        RHS = cut(bigD, 4240, (2, NT, 3))
        OH = cut(bigC, 4096, (2, NT, P))
        WC = bigD[:, 4260:4260 + BODY]
        NCNT = bigD[:, 4272:4273]
        IDX = sb("IDX", [P, BODY], I32)
        ROW = sb("ROW", [1, RTAB + 4], I32)
        YF = cut(bigA, 0, (NT, D))
        YN = cut(bigA, 3072, (NT, D))

        loaded = [sem(f"weights_loaded_{i}") for i in range(NSLOT)]
        in_small = sem("constants_loaded")
        in_cols = sem("small_vectors_loaded")
        in_x = sem("x_loaded")
        in_cache = sem("cache_loaded")
        in_state = sem("state_loaded")
        in_bias = [sem("bias_loaded_0"), sem("bias_loaded_1")]
        bias_masked = sem("bias_masked")
        in_xh = sem("residual_loaded")
        out_done = sem("outputs_written")
        ssq_done = sem("sum_of_squares")
        ssq_of = sem("root_mean_square")
        root_done = sem("root")
        xn_ready = sem("normed_tile")
        xnt_ready = sem("normed_transposed")
        n_ready = sem("modulated")
        unit_ready = sem("unit_ready")
        unit_taken = sem("unit_taken")
        csil_ready = sem("csilu_ready")
        modt_ready = sem("mod_transposed")
        mod_ready = sem("mod_ready")
        ck_t = sem("cache_transposed")
        ck_taken = sem("cache_t_taken")
        s_ready = sem("scores_ready")
        s_taken = sem("scores_taken")
        max_ready = sem("max_ready")
        exp_ready = sem("exp_ready")
        prob_ready = sem("probs_ready")
        pt_ready = sem("probs_transposed")
        pt_taken = sem("probs_t_taken")
        pv_ready = sem("values_ready")
        pv_taken = sem("values_taken")
        conv_done = sem("conv_done")
        sig_done = sem("gate_sigmoids")
        f_done = sem("forget_ready")
        logf_done = sem("logf_ready")
        b_done = sem("decay_sums")
        diff_done = sem("level_diff")
        edec_done = sem("level_decay")
        qk_done = sem("level_operands")
        lev_ready = sem("level_products")
        lev_taken = sem("level_taken")
        kh_done = sem("carry_keys")
        kht_ready = sem("carry_keys_t")
        kht_taken = sem("carry_keys_t_taken")
        kv_ready = sem("carry_products")
        st_done = sem("states_done")
        ho_ready = sem("hgrn_out_ready")
        ho_taken = sem("hgrn_out_copied")
        ho_ms = sem("hgrn_mean_square")
        ho_root = sem("hgrn_root")
        ho_norm = sem("hgrn_normed")
        hot_ready = sem("hgrn_out_t")
        hot_taken = sem("hgrn_out_t_taken")
        late_done = sem("late_sigmoids")
        gb_ready = sem("gate_rows_spread")
        gb_taken = sem("gate_rows_taken")
        br_ready = sem("branch_products")
        br_taken = sem("branch_taken")
        mix_done = sem("mix_done")
        wo_ready = sem("out_products")
        wo_taken = sem("out_taken")
        dve_order = sem("dve_order")
        prep_order = sem("prep_order")
        act_order = sem("act_order")
        pool_order = sem("pool_order")
        gather_go = sem("gather_may_start")
        added = sem("results_added_through")
        sh_loaded = sem("shared_weights_loaded")
        bg_loaded = sem("gate_bias_loaded")
        gr_ready = sem("gate_rows_ready")
        state_out = sem("states_written")
        cache_out = sem("caches_written")
        fin_loaded = sem("final_weights_loaded")
        ssq2 = sem("sum_of_squares_2")
        ms2 = sem("mean_square_2")
        root2 = sem("root_2")
        xn2 = sem("normed_2")
        xnt2 = sem("normed_transposed_2")
        n2_ready = sem("modulated_2")
        n2t_ready = sem("rows_2_in_psum")
        n2_rowed = sem("rows_2_copied")
        n2_out = sem("rows_2_written")
        rt_ready = sem("router_logits")
        rt_sig = sem("router_sigmoids")
        mask_ready = sem("expert_mask")
        pos_ready = sem("positions_counts")
        tab_ready = sem("round_table_operands")
        te_ready = sem("table_transposed")
        te_taken = sem("table_transposed_taken")
        pr_ready = sem("round_positions")
        comb_done = sem("round_weights_taken")
        row_done = sem("round_row")
        sg_ready = sem("shared_gate_up")
        ss_done = sem("shared_silu")
        sh_hid = sem("shared_hidden")
        sht_ready = sem("shared_hidden_t")
        sht_taken = sem("shared_hidden_t_taken")
        shd_ready = sem("shared_down")
        sho_done = sem("shared_out")
        y_init = sem("y_rows_initialised")
        gu_loaded = [sem(f"gate_up_loaded_{i}") for i in range(WS)]
        dn_loaded = [sem(f"down_loaded_{i}") for i in range(WS)]
        oh_done = sem("one_hots")
        ix_ready = sem("index_products")
        idx_done = sem("indices")
        gathered = [sem(f"gathered_{i}") for i in range(XGS)]
        xg_t = sem("gathered_t")
        xt_done = sem("gathered_t_taken")
        gu_ready = sem("gate_up_products")
        silu_done = sem("silu")
        hid_done = sem("hidden")
        ht_ready = sem("hidden_t")
        ht_done = sem("hidden_t_taken")
        dn_ready = sem("down_products")
        ys_done = sem("results_weighted")
        scat = sem("results_added")
        y_back = sem("sums_loaded")
        h2_done = sem("residual_2")
        fin_done = sem("final_normed")

        block = ctx.enter_context(nc.Block())

        def arrived(eng, key):
            n = SLOT_OF[key]
            eng.wait_ge(loaded[n % NSLOT], 16 * (n // NSLOT + 1))

        def slot(key):
            return ring[:, SLOT_OF[key] % NSLOT, :]

        def free_after(eng, key):
            src, i = key
            if src == "ada":
                eng.wait_ge(unit_ready, AFTER[("ada", i)])
            elif src == "in":
                eng.wait_ge(unit_ready, AFTER[IN_CHUNKS[i]])
            elif src == "br":
                eng.wait_ge(br_ready, 24)
            elif src == "out":
                eng.wait_ge(wo_ready, 2 * NT)

        def round_count(eng):
            eng.wait_ge(row_done, 1)
            return ROW[0:1, RTAB:RTAB + 1]

        @block.sync
        def _(sp):
            sp.dma_start(C[:], cols).then_inc(in_cols, 16)
            wi = w_in.rearrange("(p k) n -> p k n", k=KD)
            wa = w_ada.rearrange("(p k) n -> p k n", k=KD)
            order = {"q": 0, "k": 1, "v": 2, "u": 3, "gb": 4, "gc": 5, "qc": 6, "zf": 7, "zb": 8, "ic": 9, "oc": 10}
            for n, (src, i) in enumerate(STREAM):
                if n == 2:
                    sp.dma_start(X, x.rearrange("(m p) d -> p m d", p=P)).then_inc(in_x, 16)
                    sp.dma_start(K[:], consts).then_inc(in_small, 16)
                if n >= NSLOT:
                    free_after(sp, STREAM[n - NSLOT])
                dst = ring[:, n % NSLOT, :]
                if src == "ada":
                    a = wa[:, :, i * WCH:(i + 1) * WCH]
                    sp.dma_start(dst.rearrange("p (k n) -> p k n", k=KD), a).then_inc(loaded[n % NSLOT], 16)
                elif src == "in":
                    i = order.get(IN_CHUNKS[i], i)
                    a = wi[:, :, i * WCH:(i + 1) * WCH]
                    sp.dma_start(dst.rearrange("p (k n) -> p k n", k=KD), a).then_inc(loaded[n % NSLOT], 16)
                elif src == "br":
                    a = w_br[i].rearrange("(k p) n -> p k n", p=P)
                    sp.dma_start(dst.rearrange("p (k n) -> p k n", k=4), a).then_inc(loaded[n % NSLOT], 16)
                elif src == "out":
                    a = w_out.rearrange("(k p) n -> p k n", p=P)[:, :, i * WCH:(i + 1) * WCH]
                    sp.dma_start(dst.rearrange("p (k n) -> p k n", k=KD), a).then_inc(loaded[n % NSLOT], 16)
                elif src == "sh":
                    d3 = dst.rearrange("p (k n) -> p k n", k=KD)
                    sp.dma_start(d3[:, :, 0:DE], w_sh_gate.rearrange("(p k) n -> p k n", k=KD)).then_inc(sh_loaded, 16)
                    sp.dma_start(d3[:, :, DE:2 * DE], w_sh_up.rearrange("(p k) n -> p k n", k=KD)).then_inc(sh_loaded, 16)
                else:
                    sp.dma_start(dst[:, 0:2 * D].rearrange("p (k n) -> p k n", k=2),
                                 w_sh_down.rearrange("(k p) n -> p k n", p=P)).then_inc(sh_loaded, 16)
            sp.wait_ge(gb_taken, 8)
            sp.dma_start(WR, w_router.rearrange("(p k) e -> p k e", k=KD)).then_inc(fin_loaded, 16)
            sp.dma_start(BR, b_router.partition_broadcast(P)).then_inc(fin_loaded, 16)
            sp.wait_ge(br_ready, 24)
            sp.dma_start(FG, final_g.partition_broadcast(P)).then_inc(fin_loaded, 16)

            wg = w_gate.rearrange("e (p k) n -> e p k n", k=KD)
            wu = w_up.rearrange("e (p k) n -> e p k n", k=KD)
            wd = w_down.rearrange("e (k p) n -> e p k n", p=P)

            def experts(r, q):
                e = sp.value_load(ROW[0:1, bass.ds(r, 1)], min_val=0, max_val=NE - 1)
                one = lambda a: a[bass.ds(e, 1)].rearrange("o p k n -> p (o k) n")
                sp.dma_start(GU_W[q][:, :, 0:DE], one(wg)).then_inc(gu_loaded[q], 16)
                sp.dma_start(GU_W[q][:, :, DE:2 * DE], one(wu)).then_inc(gu_loaded[q], 16)
                sp.dma_start(DN_W[q], one(wd)).then_inc(dn_loaded[q], 16)

            sp.wait_ge(row_done, 1)
            rounds = sp.value_load(round_count(sp), min_val=1, max_val=ROUNDS)
            sp.wait_ge(n2_out, 32)
            experts(0, 0)
            sp.wait_ge(shd_ready, NT)
            experts(1, 1)
            experts(2, 2)
            with sp.Fori(0, PASSES) as pas:
                for p in range(BODY):
                    i = pas * BODY + (1 + p)
                    with sp.If(i + 2 <= rounds):
                        sp.wait_ge(dn_ready, i)
                        experts(i + 2, p % WS)
            sp.wait_ge(scat, rounds * 16 + 16)
            sp.dma_start(YF, y_rows[0:T, :].rearrange("(m p) d -> p m d", p=P)).then_inc(y_back, 16)
            for m in range(NT):
                sp.wait_ge(fin_done, m + 1)
                sp.dma_start(y[m * P:(m + 1) * P, :], YN[:, m, :]).then_inc(out_done, 16)
            sp.wait_ge(out_done, 16 * NT)
            sp.wait_ge(cache_out, 32)
            sp.wait_ge(state_out, 32)

        @block.scalar
        def _(act):
            chain = [0]

            def link(ins):
                chain[0] += 1
                ins.then_inc(act_order, 1)
                act.wait_ge(act_order, chain[0])

            act.dma_start(CK, cache_k).then_inc(in_cache, 16)
            act.dma_start(CV, cache_v).then_inc(in_cache, 16)
            for ev in SCHEDULE:
                st = ev[0]
                if st == "norm1":
                    act.wait_ge(in_cols, 16)
                    nc.scalar.activation(csil[:, :, :].rearrange("p k v -> p v k"),
                                         cc(C_C).rearrange("p (v k) -> p v k", v=2), ACT.Silu).then_inc(csil_ready, 1)
                    act.wait_ge(in_x, 16)
                    for m in range(NT):
                        nc.scalar.activation(XN[:, m, :], X[:, m, :], ACT.Square,
                                             accum_out=small[:, m:m + 1]).then_inc(ssq_done, 1)
                    act.wait_ge(ssq_of, 1)
                    nc.scalar.activation(small[:, 8:8 + NT], small[:, 4:4 + NT], ACT.Sqrt).then_inc(root_done, 1)
                elif st == "unit":
                    n = ev[1]
                    name, c, j = UNITS[n]
                    ps = PS[:, n % 2, :]
                    act.wait_ge(unit_ready, n + 1)
                    if name == "g0":
                        act.wait_ge(cache_out, 32)
                    if name == "ada":
                        if c < 4:
                            out = ADA[0:2, c * WCH:(c + 1) * WCH]
                        elif c < 6:
                            if c == 4:
                                act.wait_ge(st_done, 3)
                            out = GR[0:2, (c - 4) * WCH:(c - 3) * WCH]
                        elif c < 10:
                            out = Zrows[:, (c - 6) * WCH:(c - 5) * WCH]
                        else:
                            out = GR[0:2, (c - 8) * WCH:(c - 7) * WCH]
                        nc.scalar.activation(out, ps[0:2, :], ACT.Copy).then_inc(unit_taken, 1)
                        continue
                    if name == "v":
                        act_out, src = V[:, j, :], ps
                    elif name == "ic":
                        act_out, src = IC[:, j, :], ps
                    elif name == "q":
                        nc.scalar.activation(Q[:, j, 0:CTX], ps[:, 0:CTX], ACT.Copy, scale=DH ** -0.5)
                        act_out = Q[:, j, CTX:T].rearrange("p (r c) -> p r c", c=GRID_W)[:, :, ::-1]
                        src = ps[:, CTX:T].rearrange("p (r c) -> p r c", c=GRID_W)
                        nc.scalar.activation(act_out, src, ACT.Copy, scale=DH ** -0.5).then_inc(unit_taken, 1)
                        continue
                    else:
                        src = ps[:, 0:T]
                        if name == "k":
                            act_out = KT[:, j, :]
                        elif name == "u":
                            act_out = UU[:, j, :]
                        elif name == "gb":
                            act_out = GB[:, j, :]
                        elif name == "gc":
                            act_out = GC[:, j, 0:T]
                        elif name == "qc":
                            act_out = QC[:, j, :]
                        elif name == "zf":
                            act_out = Z[:, 0, j, :]
                        elif name == "zb":
                            act_out = Z[:, 1, j, :]
                        elif name == "oc":
                            act_out = OG[:, j, :]
                        else:
                            act_out = G[:, (c - 11) * 4 + j, :]
                    nc.scalar.activation(act_out, src, ACT.Copy).then_inc(unit_taken, 1)
                elif st == "cache":
                    act.wait_ge(ck_t, 1)
                    nc.scalar.activation(CKT.rearrange("p j t -> p (j t)"), PS[:, 4, :], ACT.Copy).then_inc(ck_taken, 1)
                    act.wait_ge(ck_t, 2)
                    nc.scalar.activation(CKO, PS[:, 5, :], ACT.Copy).then_inc(ck_taken, 1)
                    act.wait_ge(ck_taken, 2)
                    act.dma_start(new_k, CKO).then_inc(cache_out, 16)
                    act.wait_ge(unit_taken, AFTER["v"])
                    act.dma_start(new_v, V[:, 0, :]).then_inc(cache_out, 16)
                elif st == "scores":
                    h = ev[1]
                    for u in range(3):
                        i = 3 * h + u
                        act.wait_ge(max_ready, i + 1)
                        w = P if u == 2 else T
                        if h > 0 and u == 0:
                            act.wait_ge(pt_ready, 3 * h)
                        nc.scalar.activation(PR[:, u, 0:w], SB[:, u, 0:w], ACT.Exp, bias=small[:, 16 + u:17 + u],
                                             accum_out=small[:, 20 + u:21 + u]).then_inc(exp_ready, 1)
                elif st == "values":
                    h = ev[1]
                    for u in range(3):
                        i = 3 * h + u
                        act.wait_ge(pt_ready, i + 1)
                        if u == 0 and h > 0:
                            act.wait_ge(pv_ready, h)
                        if u < 2:
                            nc.scalar.activation(PT[:, :, u * P:(u + 1) * P],
                                                 PS[:, 4, 0:T].rearrange("p (k t) -> p k t", k=3), ACT.Copy).then_inc(pt_taken, 1)
                        else:
                            nc.scalar.activation(PTC, PS[:, 4, 0:P], ACT.Copy).then_inc(pt_taken, 1)
                    o = 64 * (h % 2)
                    act.wait_ge(pv_ready, h + 1)
                    nc.scalar.activation(OA[o:o + DH, h // 2, CTX:T].rearrange("p (r c) -> p r c", c=GRID_W)[:, :, ::-1],
                                         PS[o:o + DH, 5, 0:2 * P].rearrange("p (r c) -> p r c", c=GRID_W),
                                         ACT.Copy)
                    nc.scalar.activation(OA[o:o + DH, h // 2, 0:CTX], PS[o:o + DH, 5, 2 * P:3 * P], ACT.Copy).then_inc(pv_taken, 1)
                elif st == "gates":
                    act.wait_ge(conv_done, 1)
                    act.wait_ge(pv_ready, NH)
                    for d in range(2):
                        act.dma_start(ST[:, d, :, :], state[d].rearrange("h k v -> k h v")).then_inc(in_state, 16)
                    act.wait_ge(unit_taken, AFTER["zb"])
                    link(nc.scalar.activation(KEY, Z, ACT.Sigmoid, scale=-1.0))
                    nc.scalar.activation(Z, Z, ACT.Sigmoid).then_inc(sig_done, 1)
                elif st == "decays":
                    act.wait_ge(f_done, 1)
                    nc.scalar.activation(Z, Z, ACT.Ln).then_inc(logf_done, 1)
                elif st == "ops":
                    if ev[1] % 8 < 7:
                        act.wait_ge(diff_done, ev[1] - ev[1] // 8 + 1)
                        nc.scalar.activation(E, E, ACT.Exp).then_inc(edec_done, 1)
                elif st == "carry":
                    act.wait_ge(diff_done, 15)
                    act.wait_ge(b_done, 1)
                    link(nc.scalar.activation(KH, KH, ACT.Exp))
                    nc.scalar.activation(EB, Z[:, :, :, CTX:T], ACT.Exp).then_inc(edec_done, 1)
                elif st == "carry_t":
                    for c in range(4):
                        act.wait_ge(kht_ready, c + 1)
                        nc.scalar.activation(KHT[:, c, :, :].rearrange("p h t -> p (h t)"), PS[:, 4 + c % 2, :],
                                             ACT.Copy).then_inc(kht_taken, 1)
                elif st == "hout":
                    m = ev[1]
                    act.wait_ge(ho_ready, m + 1)
                    if m > 0:
                        act.wait_ge(ho_norm, m)
                    nc.scalar.activation(OS, PS[:, 6, :], ACT.Copy).then_inc(ho_taken, 1)
                    act.wait_ge(ho_ms, m + 1)
                    nc.scalar.activation(small[:, 36:40], small[:, 32:36], ACT.Sqrt).then_inc(ho_root, 1)
                    if m == 0:
                        act.wait_ge(unit_taken, AFTER["oc"])
                        nc.scalar.activation(OG, OG, ACT.Silu).then_inc(late_done, 1)
                        for d in range(2):
                            act.dma_start(new_state[d].rearrange("h k v -> k h v"), STC[:, d, :, :]).then_inc(state_out, 16)
                elif st == "late_act":
                    b = ev[1]
                    if b == 0:
                        act.wait_ge(unit_taken, AFTER["g5"])
                        act.wait_ge(ho_ready, NT)
                        act.dma_start(XH, x.rearrange("(m p) d -> p m d", p=P)).then_inc(in_xh, 16)
                        act.dma_start(BG[0:2, :], b_gate).then_inc(bg_loaded, 16)
                    g = G[:, 8 * b:8 * b + 8, :]
                    nc.scalar.activation(g, g, ACT.Sigmoid).then_inc(late_done, 1)
                elif st == "norm2":
                    act.wait_ge(wo_taken, 2 * NT)
                    for m in range(NT):
                        nc.scalar.activation(XN2[:, m, :], XH[:, m, :], ACT.Square,
                                             accum_out=small[:, m:m + 1]).then_inc(ssq2, 1)
                    act.wait_ge(ms2, 1)
                    nc.scalar.activation(small[:, 8:8 + NT], small[:, 4:4 + NT], ACT.Sqrt).then_inc(root2, 1)
                    for i in range(2 * NT):
                        m, hf = i // 2, i % 2
                        act.wait_ge(n2t_ready, i + 1)
                        dst = N2[:, m, :].rearrange("p (f k) -> p k f", k=KD)[:, 4 * hf:4 * hf + 4, :]
                        nc.scalar.activation(dst, PS[:, 6 + i % 2, :].rearrange("p (k f) -> p k f", k=4), ACT.Copy).then_inc(n2_rowed, 1)
                    act.wait_ge(n2_rowed, 2 * NT)
                    act.dma_start(n2_rows[0:T, :].rearrange("(m p) d -> p m d", p=P), N2).then_inc(n2_out, 16)
                    act.dma_start(n2_rows[T:T + P, :], N2[:, 0, :]).then_inc(n2_out, 16)
                elif st == "router":
                    act.wait_ge(rt_ready, 1)
                    nc.scalar.activation(SG, PS[:, 6, 0:NT * NE].rearrange("p (m e) -> p m e", m=NT), ACT.Sigmoid).then_inc(rt_sig, 1)
                elif st == "table":
                    act.wait_ge(te_ready, 1)
                    nc.scalar.activation(TE[0:NE, 0:4, :], PS[0:NE, 6, :].rearrange("p (a t) -> p a t", a=4), ACT.Copy)
                    nc.scalar.activation(TE[0:NE, 4:7, :], PS[0:NE, 7, 0:T].rearrange("p (a t) -> p a t", a=3), ACT.Copy).then_inc(te_taken, 1)
                    act.wait_ge(pr_ready, 1)
                    nc.scalar.activation(COMB, PS[:, 3, 0:T].rearrange("p (m r) -> p m r", m=NT), ACT.Copy).then_inc(comb_done, 1)
                elif st == "shared":
                    m = ev[1]
                    act.wait_ge(sg_ready, m + 1)
                    nc.scalar.activation(HS[:, m % 2, :], PS[:, 4 + m % 2, 0:DE], ACT.Silu).then_inc(ss_done, 1)
                    act.wait_ge(sht_ready, m + 1)
                    nc.scalar.activation(HT[:, m % 2, :, :], PS[:, 0, 0:2 * P].rearrange("p (k t) -> p k t", k=2), ACT.Copy).then_inc(sht_taken, 1)
                    act.wait_ge(shd_ready, m + 1)
                    nc.scalar.activation(SHO[:, m, :].rearrange("p (a n) -> p a n", a=2), PS[:, 1:3, :], ACT.Copy).then_inc(sho_done, 1)
                    if m == NT - 1:
                        act.wait_ge(sho_done, NT)
                        act.dma_start(y_rows[0:T, :].rearrange("(m p) d -> p m d", p=P), SHO).then_inc(y_init, 16)

            def take_xt(r, b):
                act.wait_ge(xg_t, r + 1)
                nc.scalar.activation(XT[:, b, :, :].rearrange("p (a k) t -> p a (k t)", a=2), PS[:, 0:2, :], ACT.Copy).then_inc(xt_done, 1)

            def silu(r, b):
                act.wait_ge(gu_ready, r + 1)
                nc.scalar.activation(HS[:, b, :], PS[:, 2 + b, 0:DE], ACT.Silu).then_inc(silu_done, 1)

            rounds = act.value_load(round_count(act), min_val=1, max_val=ROUNDS)
            take_xt(0, 0)
            take_xt(1, 1)
            silu(0, 0)
            with act.Fori(0, PASSES) as pas:
                for p in range(BODY):
                    i = pas * BODY + (1 + p)
                    with act.If(i <= rounds):
                        act.wait_ge(gu_ready, i)
                        take_xt(i + 1, p % 2)
                        act.wait_ge(ht_ready, i)
                        nc.scalar.activation(HT[:, p % 2, :, :], PS[:, 5, 0:2 * P].rearrange("p (k t) -> p k t", k=2),
                                             ACT.Copy).then_inc(ht_done, 1)
                        act.wait_ge(hid_done, i)
                        silu(i, (1 + p) % 2)
            act.wait_ge(h2_done, NT)
            for m in range(NT):
                nc.scalar.activation(YN[:, m, :], YF[:, m, :], ACT.Square, accum_out=small[:, m:m + 1]).then_inc(ssq2, 1)
            act.wait_ge(ms2, 2)
            nc.scalar.activation(small[:, 8:8 + NT], small[:, 4:4 + NT], ACT.Sqrt).then_inc(root2, 1)

        @block.gpsimd
        def _(pool):
            chain = [0]

            def link(ins):
                chain[0] += 1
                ins.then_inc(pool_order, 1)
                pool.wait_ge(pool_order, chain[0])

            link(nc.gpsimd.memset(BIAS, 0.0))
            pool.wait_ge(in_small, 16)
            for h in range(NH):
                b = h % 2
                if h >= 2:
                    pool.wait_ge(s_taken, 3 * (h - 1))
                for qr in range(4):
                    src = bass.AP(rpb.tensor, h * 15 * 31 + (7 - qr) * 31 - 48, [[1, GRID_W], [31, 4], [1, GRID_W]])
                    o = 64 * (qr % 2)
                    pool.dma_start(BIAS[o:o + 64, b, qr // 2, 0:256].rearrange("p (r c) -> p r c", r=4), src)\
                        .then_inc(in_bias[b], 16)
                pool.wait_ge(in_bias[b], 64 * (h // 2 + 1))
                for t in range(2):
                    v = BIAS[:, b, t, 0:256].rearrange("p (r c) -> p r c", r=4)
                    nc.gpsimd.tensor_tensor(v, v, kc(K_MASK).unsqueeze(1).broadcast_to([P, 4, GRID_W]), ALU.add)\
                        .then_inc(bias_masked, 1)

            def gather(r, p):
                pool.wait_ge(idx_done, r + 1)
                pool.sem_inc(gather_go, 1)
                pool.indirect_dma_start(XG[:, p % XGS, :], None, n2_rows,
                                        bass.IndirectOffsetOnAxis(ap=IDX[:, p:p + 1], axis=0)).then_inc(gathered[p % XGS], 16)

            pool.wait_ge(n2_out, 32)
            for r in range(XGS):
                gather(r, r)
            pool.wait_ge(xg_t, 1)
            gather(XGS, XGS)
            pool.wait_ge(sho_done, 1)
            pool.dma_start(y_rows[T:T + P, :], SHO[:, 0, :]).then_inc(scat, 16)
            pool.wait_ge(y_init, 16)
            pool.sem_inc(added, 1)
            rounds = pool.value_load(round_count(pool), min_val=1, max_val=ROUNDS)
            with pool.Fori(0, PASSES) as pas:
                for p in range(BODY):
                    i = pas * BODY + (1 + p)
                    with pool.If(i <= rounds):
                        pool.wait_ge(xg_t, i + 1)
                        gather(i + AHEAD, (1 + p + AHEAD) % BODY)
                        pool.wait_ge(ys_done, i + 1)
                        pool.wait_ge(scat, 16 * i)
                        pool.sem_inc(added, 1)
                        pool.indirect_dma_start(y_rows, bass.IndirectOffsetOnAxis(ap=IDX[:, p:p + 1], axis=0),
                                                YS[:, p % 2, :], None, compute_op=ALU.add).then_inc(scat, 16)


        @block.vector
        def _(dve):
            chain = [0]

            def link(ins):
                chain[0] += 1
                ins.then_inc(dve_order, 1)
                dve.wait_ge(dve_order, chain[0])

            def rsqrt_fix(ms, root, r, t):
                link(nc.vector.reciprocal(r, root))
                link(nc.vector.tensor_tensor(t, r, r, ALU.mult))
                link(nc.vector.tensor_tensor(t, t, ms, ALU.mult))
                link(nc.vector.tensor_scalar(t, t, -0.5, 1.5, ALU.mult, ALU.add))
                link(nc.vector.tensor_tensor(r, r, t, ALU.mult))

            def prep(r, p):
                b = p % 2
                dve.wait_ge(idx_done, r)
                for m in range(NT):
                    nc.vector.tensor_scalar(OH[:, b, m, :], kc(K_R128), POSR[:, m, bass.ds(r, 1)], None, ALU.is_equal)
                nc.vector.tensor_copy(RHS[:, b, :, 2:3], COMB[:, :, bass.ds(r, 1)]).then_inc(oh_done, 1)
                dve.wait_ge(ix_ready, r + 1)
                ix = PS[:, 4, 0:3]
                link2(nc.vector.tensor_scalar(NCNT, ix[:, 1:2], -1.0, 1.0, ALU.mult, ALU.add), r + 1)
                nc.vector.tensor_copy(WC[:, p:p + 1], ix[:, 2:3])
                nc.vector.scalar_tensor_tensor(IDX[:, p:p + 1], NCNT, kc(K_COL)[:, 1:2], ix[:, 0:1],
                                               ALU.mult, ALU.add).then_inc(idx_done, 1)

            def link2(ins, n):
                ins.then_inc(prep_order, 1)
                dve.wait_ge(prep_order, n)

            def modulate(which, ready, done):
                for k in range(KD):
                    dve.wait_ge(ready, k + 1)
                    nc.vector.tensor_scalar(nT[:, k, 0:CTX], PS[:, 2 + k % 4, 0:CTX], modc[:, which + 1, 0, k:k + 1],
                                            modc[:, which, 0, k:k + 1], ALU.mult, ALU.add).then_inc(dve_order, 1)
                    chain[0] += 1
                    nc.vector.tensor_scalar(nT[:, k, CTX:T], PS[:, 2 + k % 4, CTX:T], modc[:, which + 1, 1, k:k + 1],
                                            modc[:, which, 1, k:k + 1], ALU.mult, ALU.add).then_inc(done, 1)
                dve.wait_ge(done, KD)
                dve.wait_ge(dve_order, chain[0])

            def mod_columns(which, bank, nvec, norm, cnt):
                src = PS[:, bank, 0:32].rearrange("p (s k v) -> p s v k", s=2, v=2)
                b = cc(C_ADA).rearrange("p (s k) -> p s k", s=4)
                for s in range(2):
                    link(nc.vector.tensor_tensor(modc[:, which + s, :, :], src[:, s, :, :],
                                                 b[:, which + s, :].unsqueeze(1).broadcast_to([P, 2, KD]), ALU.add))
                link(nc.vector.tensor_scalar(modc[:, which + 1, :, :], modc[:, which + 1, :, :], 1.0, None, ALU.add))
                nc.vector.tensor_tensor(modc[:, which + 1, :, :], modc[:, which + 1, :, :],
                                        norm.unsqueeze(1).broadcast_to([P, 2, KD]), ALU.mult).then_inc(mod_ready, 1)
                dve.wait_ge(mod_ready, cnt)

            def take_level(i):
                dve.wait_ge(lev_ready, i + 1)
                if i > 0:
                    dve.wait_ge(lev_taken, i)
                mask = levmask[:, i % 8, :] if i % 8 < 7 else ident.bitcast(U32)
                for hh in range(2):
                    ins = nc.vector.copy_predicated(AT_[:, 2 * (i // 8) + hh, :, :], mask.unsqueeze(1).broadcast_to([P, NT, P]),
                                                    PS[:, 6 + hh, 0:T].rearrange("p (m t) -> p m t", m=NT))
                ins.then_inc(lev_taken, 1)

            dve.sem_inc(hid_done, 1)
            dve.sem_inc(ys_done, 1)
            for ev in SCHEDULE:
                st = ev[0]
                if st == "norm1":
                    dve.wait_ge(ssq_done, NT)
                    nc.vector.tensor_scalar(small[:, 4:4 + NT], small[:, 0:NT], 1.0 / D, EPS, ALU.mult, ALU.add).then_inc(ssq_of, 1)
                    dve.wait_ge(ssq_of, 1)
                    dve.wait_ge(root_done, 1)
                    rsqrt_fix(small[:, 4:4 + NT], small[:, 8:8 + NT], small[:, 12:12 + NT], small[:, 24:24 + NT])
                    for m in range(NT):
                        nc.vector.tensor_scalar(XN[:, m, :], X[:, m, :], small[:, 12 + m:13 + m], None, ALU.mult).then_inc(xn_ready, 1)
                elif st == "mod1":
                    dve.wait_ge(in_cols, 16)
                    dve.wait_ge(modt_ready, 1)
                    mod_columns(0, 7, 2, cc(C_N1), 1)
                    modulate(0, xnt_ready, n_ready)
                elif st == "scores":
                    h = ev[1]
                    for u in range(3):
                        i = 3 * h + u
                        dve.wait_ge(s_ready, i + 1)
                        if h > 0:
                            dve.wait_ge(exp_ready, 3 * h)
                        if u < 2:
                            dve.wait_ge(bias_masked, 2 * h + 2)
                            nc.vector.tensor_tensor(SB[:, u, :], PS[:, 2 + i % 2, 0:T], BIAS[:, h % 2, u, :], ALU.add).then_inc(s_taken, 1)
                            w = T
                        else:
                            nc.vector.tensor_copy(SB[:, 2, 0:P], PS[:, 2 + i % 2, 0:P]).then_inc(s_taken, 1)
                            w = P
                        dve.wait_ge(s_taken, i + 1)
                        nc.vector.tensor_reduce(small[:, 16 + u:17 + u], SB[:, u, 0:w], AX.X, ALU.max,
                                                negate=True).then_inc(max_ready, 1)
                    for u in range(3):
                        i = 3 * h + u
                        w = P if u == 2 else T
                        dve.wait_ge(exp_ready, i + 1)
                        link(nc.vector.reciprocal(small[:, 28 + u:29 + u], small[:, 20 + u:21 + u]))
                        nc.vector.tensor_scalar(PR[:, u, 0:w], PR[:, u, 0:w], small[:, 28 + u:29 + u], None,
                                                ALU.mult).then_inc(prob_ready, 1)
                    dve.wait_ge(prob_ready, 3 * h + 3)
                elif st == "conv":
                    dve.wait_ge(unit_taken, AFTER["gc"])
                    link(nc.vector.memset(ZP, 0.0))
                    link(nc.vector.tensor_tensor(ZP[:, :, 1:1 + CTX], GC[:, :, 0:CTX], UU[:, :, 0:CTX], ALU.mult))
                    link(nc.vector.tensor_tensor(ZP[:, :, 3 + CTX:3 + T], GC[:, :, CTX:T], UU[:, :, CTX:T], ALU.mult))
                    wv = cc(C_CONV).rearrange("p (w j) -> p w j", w=3)
                    for j in range(4):
                        acc = GC[:, j, 1:387]
                        link(nc.vector.tensor_scalar(acc, ZP[:, j, 1:387], wv[:, 1, j:j + 1], None, ALU.mult))
                        link(nc.vector.scalar_tensor_tensor(acc, ZP[:, j, 0:386], wv[:, 0, j:j + 1], acc, ALU.mult, ALU.add))
                        link(nc.vector.scalar_tensor_tensor(acc, ZP[:, j, 2:388], wv[:, 2, j:j + 1], acc, ALU.mult, ALU.add))
                    link(nc.vector.tensor_tensor(GB[:, :, 0:CTX], GB[:, :, 0:CTX], GC[:, :, 1:1 + CTX], ALU.mult))
                    nc.vector.tensor_tensor(GB[:, :, CTX:T], GB[:, :, CTX:T], GC[:, :, 3 + CTX:3 + T], ALU.mult).then_inc(conv_done, 1)
                    dve.wait_ge(conv_done, 1)
                elif st == "gates":
                    lbr, lb = cc(C_LB), small[:, 48:56]
                    omlb, lbf, e8 = small[:, 56:64], small[:, 64:72], small[:, 72:80]
                    link(nc.vector.tensor_tensor(lb, lbr, lbr, ALU.subtract))
                    link(nc.vector.tensor_scalar(lb, lb, 1.0, None, ALU.add))
                    link(nc.vector.reciprocal(e8, lb))
                    link(nc.vector.tensor_tensor(e8, lb, e8, ALU.mult))
                    link(nc.vector.tensor_tensor(lb, e8, e8, ALU.subtract))
                    link(nc.vector.tensor_scalar(omlb, lb, -1.0, 1.0, ALU.mult, ALU.add))
                    link(nc.vector.tensor_scalar(lbf, lb, LOG_FLOOR, None, ALU.max))
                    dve.wait_ge(sig_done, 1)
                    for d in range(2):
                        for h in range(HC):
                            q = 4 * d + h
                            nc.vector.tensor_scalar(KEY[:, d, h, :], KEY[:, d, h, :], omlb[:, q:q + 1], None, ALU.mult).then_inc(dve_order, 1)
                            nc.vector.tensor_scalar(Z[:, d, h, :], Z[:, d, h, :], omlb[:, q:q + 1], lbf[:, q:q + 1],
                                                    ALU.mult, ALU.add).then_inc(dve_order, 1)
                            chain[0] += 2
                    dve.wait_ge(dve_order, chain[0])
                    link(nc.vector.tensor_copy(small[:, 80:81], small[:, 56:57]))
                    nc.vector.tensor_copy(small[:, 81:82], small[:, 56:57]).then_inc(f_done, 1)
                elif st == "decays":
                    dve.wait_ge(logf_done, 1)
                    scan = kc(K_SCAN)
                    for h in range(HC):
                        nc.vector.tensor_tensor_scan(Z[:, 0, h, :], scan, Z[:, 0, h, :], 0.0, ALU.mult, ALU.add).then_inc(dve_order, 1)
                        nc.vector.tensor_tensor_scan(Z[:, 1, h, ::-1], scan, Z[:, 1, h, ::-1], 0.0, ALU.mult, ALU.add).then_inc(dve_order, 1)
                        chain[0] += 2
                    dve.wait_ge(dve_order, chain[0])
                    nc.vector.tensor_copy(small[:, 82:83], small[:, 56:57]).then_inc(b_done, 1)
                elif st == "ops":
                    i = ev[1]
                    h2, l = i // 8, i % 8
                    hs = slice(2 * h2, 2 * h2 + 2)
                    if i == 0:
                        dve.wait_ge(pv_ready, NH)
                        dve.wait_ge(cache_out, 32)
                        link(nc.vector.memset(AT_, 0.0))
                    else:
                        dve.wait_ge(qk_done, i)
                    if l < 7:
                        L = LEVELS[l]
                        nb, hf = 2 * T // L, L // 2
                        cutb = lambda a: a.rearrange("p (n l) -> p n l", l=L)
                        zz = [Z[:, d, hs, :].rearrange("p h t -> p (h t)") for d in range(2)]
                        ref = [cutb(zz[0])[:, :, hf - 1:hf], cutb(zz[1])[:, :, hf:hf + 1]]
                        for d, right in ((0, True), (0, False), (1, True), (1, False)):
                            s = slice(hf, L) if right else slice(0, hf)
                            tok, mid = cutb(zz[d])[:, :, s], ref[d].broadcast_to([P, nb, hf])
                            a, c = (tok, mid) if right == (d == 0) else (mid, tok)
                            ins = nc.vector.tensor_tensor(cutb(E[:, d, :])[:, :, s], a, c, ALU.subtract)
                        ins.then_inc(diff_done, 1)
                    if i > 0:
                        take_level(i - 1)
                    if l < 7:
                        dve.wait_ge(edec_done, 7 * h2 + l + 1)
                        qq = QC[:, hs, :].rearrange("p h t -> p (h t)")
                        kk = [KEY[:, d, hs, :].rearrange("p h t -> p (h t)") for d in range(2)]
                        for out, a, d, right in ((QX, qq, 0, True), (QX, qq, 1, False), (KX, kk[1], 1, True), (KX, kk[0], 0, False)):
                            s = slice(hf, L) if right else slice(0, hf)
                            ins = nc.vector.tensor_tensor(cutb(out)[:, :, s], cutb(a)[:, :, s],
                                                          cutb(E[:, d, :])[:, :, s], ALU.mult)
                    else:
                        nc.vector.tensor_copy(QX, QC[:, hs, :].rearrange("p h t -> p (h t)"))
                        ins = nc.vector.tensor_tensor(KX, KEY[:, 0, hs, :].rearrange("p h t -> p (h t)"),
                                                      KEY[:, 1, hs, :].rearrange("p h t -> p (h t)"), ALU.add)
                    ins.then_inc(qk_done, 1)
                elif st == "carry":
                    take_level(15)
                    for c, (d, m) in enumerate(((0, 0), (1, 0), (0, 1), (1, 2))):
                        last = m * P + (P - 1 if d == 0 else 0)
                        ins = nc.vector.tensor_tensor(KH[:, c, :, :], Z[:, d, :, last:last + 1].broadcast_to([P, HC, P]),
                                                      Z[:, d, :, m * P:(m + 1) * P], ALU.subtract)
                        if c < 3:
                            link(ins)
                        else:
                            ins.then_inc(diff_done, 1)
                    dve.wait_ge(edec_done, 15)
                    for c, (d, m) in enumerate(((0, 0), (1, 0), (0, 1), (1, 2))):
                        nc.vector.tensor_tensor(KH[:, c, :, :], KH[:, c, :, :], KEY[:, d, :, m * P:(m + 1) * P],
                                                ALU.mult).then_inc(kh_done, 1)
                elif st == "carry_products":
                    dve.wait_ge(in_state, 32)
                    for c in range(4):
                        dve.wait_ge(kv_ready, c + 1)
                        kv = PS[:, 6 + c % 2, :].rearrange("p (h v) -> p h v", h=HC)
                        if c < 2:
                            nc.vector.tensor_copy(STC[:, c, :, :], kv).then_inc(st_done, 1)
                            dve.wait_ge(st_done, c + 1)
                        else:
                            d, last = c - 2, (P - 1 if c == 2 else P)
                            for h in range(HC):
                                link(nc.vector.scalar_tensor_tensor(ST2[:, d, h, :], ST[:, d, h, :], EB[:, d, h, last:last + 1],
                                                                    kv[:, h, :], ALU.mult, ALU.add))
                    for d in range(2):
                        link(nc.vector.tensor_tensor(EB[:, d, :, :], EB[:, d, :, :], QC[:, :, CTX:T], ALU.mult))
                    nc.vector.tensor_copy(small[:, 83:84], small[:, 56:57]).then_inc(st_done, 1)
                elif st == "hout":
                    m = ev[1]
                    dve.wait_ge(ho_taken, m + 1)
                    link(nc.vector.tensor_tensor(OQ, OS, OS, ALU.mult))
                    link(nc.vector.tensor_reduce(small[:, 40:44], OQ.rearrange("p (h v) -> p h v", h=HC), AX.X, ALU.add))
                    nc.vector.tensor_scalar(small[:, 32:36], small[:, 40:44], 1.0 / P, EPS, ALU.mult, ALU.add).then_inc(ho_ms, 1)
                    dve.wait_ge(ho_ms, m + 1)
                    dve.wait_ge(ho_root, m + 1)
                    rsqrt_fix(small[:, 32:36], small[:, 36:40], small[:, 44:48], small[:, 88:92])
                    if m > 0:
                        dve.wait_ge(hot_ready, m)
                    nc.vector.tensor_tensor(OR.rearrange("p (h v) -> p h v", h=HC), OS.rearrange("p (h v) -> p h v", h=HC),
                                            small[:, 44:48].unsqueeze(2).broadcast_to([P, HC, P]), ALU.mult).then_inc(ho_norm, 1)
                elif st == "hout_t":
                    m = ev[1]
                    dve.wait_ge(late_done, 1)
                    dve.wait_ge(hot_ready, m + 1)
                    for h in range(HC):
                        ins = nc.vector.scalar_tensor_tensor(OCT[:, h, m * P:(m + 1) * P], PS[:, 7, h * P:(h + 1) * P],
                                                             cc(C_HG)[:, h:h + 1], OG[:, h, m * P:(m + 1) * P], ALU.mult, ALU.mult)
                        if h < HC - 1:
                            link(ins)
                        else:
                            ins.then_inc(hot_taken, 1)
                elif st == "mod2":
                    dve.wait_ge(state_out, 32)
                    dve.wait_ge(unit_taken, len(UNITS))
                    dve.wait_ge(modt_ready, 2)
                    mod_columns(2, 7, 2, cc(C_N2), 2)
                    dve.wait_ge(bg_loaded, 16)
                    nc.vector.tensor_tensor(GR[0:2, :], GR[0:2, :], BG[0:2, :], ALU.add).then_inc(gr_ready, 1)
                    for i in range(8):
                        g, v, hf = i // 4, i // 2 % 2, i % 2
                        dve.wait_ge(gb_ready, i + 1)
                        nc.vector.tensor_copy(GBC[:, g, v, hf * 512:(hf + 1) * 512], PS[:, 2 + i % 4, :]).then_inc(gb_taken, 1)
                elif st == "branches":
                    for i in range(24):
                        j, br = i // 3, i % 3
                        if i < 3:
                            dve.wait_ge(late_done, 2 + br)
                        dve.wait_ge(br_ready, i + 1)
                        src = PS[:, i % 6, 0:T]
                        if br == 0:
                            nc.vector.tensor_tensor(G[:, j, :], src, G[:, j, :], ALU.mult).then_inc(br_taken, 1)
                        else:
                            nc.vector.tensor_tensor(G[:, 8 * br + j, :], src, G[:, 8 * br + j, :], ALU.mult).then_inc(br_taken, 1)
                            dve.wait_ge(br_taken, i + 1)
                            ins = nc.vector.tensor_tensor(G[:, j, :], G[:, j, :], G[:, 8 * br + j, :], ALU.add)
                            if br == 1:
                                link(ins)
                            else:
                                ins.then_inc(mix_done, 1)
                elif st == "wout":
                    dve.wait_ge(in_xh, 16)
                    dve.wait_ge(gb_taken, 8)
                    for i in range(2 * NT):
                        m, hf = i // 2, i % 2
                        s = slice(hf * 512, (hf + 1) * 512)
                        dve.wait_ge(wo_ready, i + 1)
                        t = T1
                        link(nc.vector.tensor_tensor(t, PS[:, 6 + i % 2, :], GBC[:, 0, min(m, 1), s], ALU.mult))
                        nc.vector.tensor_tensor(XH[:, m, s], XH[:, m, s], t, ALU.add).then_inc(wo_taken, 1)
                        dve.wait_ge(wo_taken, i + 1)
                elif st == "norm2":
                    dve.wait_ge(ssq2, NT)
                    nc.vector.tensor_scalar(small[:, 4:4 + NT], small[:, 0:NT], 1.0 / D, EPS, ALU.mult, ALU.add).then_inc(ms2, 1)
                    dve.wait_ge(ms2, 1)
                    dve.wait_ge(root2, 1)
                    rsqrt_fix(small[:, 4:4 + NT], small[:, 8:8 + NT], small[:, 12:12 + NT], small[:, 24:24 + NT])
                    for m in range(NT):
                        nc.vector.tensor_scalar(XN2[:, m, :], XH[:, m, :], small[:, 12 + m:13 + m], None, ALU.mult).then_inc(xn2, 1)
                    modulate(2, xnt2, n2_ready)
                elif st == "router":
                    dve.wait_ge(fin_loaded, 48)
                    dve.wait_ge(rt_sig, 1)
                    link(nc.vector.tensor_tensor(SE, SG, BR.unsqueeze(1).broadcast_to([P, NT, NE]), ALU.add))
                    for m in range(NT):
                        for g in range(NG):
                            ins = nc.vector.max(M8[:, m, g, :], SE[:, m, g * 8:g * 8 + 8])
                    link(ins)
                    link(nc.vector.tensor_tensor(GS, M8[:, :, :, 0], M8[:, :, :, 1], ALU.add))
                    for m in range(NT):
                        other = GS[:, m, :].unsqueeze(1).broadcast_to([P, NG, NG])
                        own = GS[:, m, :].unsqueeze(2).broadcast_to([P, NG, NG])
                        nc.vector.tensor_tensor(CMP[:, m, :, :], other, own, ALU.is_gt)
                        ins = nc.vector.tensor_tensor(CM2[:, m, :, :], other, own, ALU.is_equal)
                    link(ins)
                    flat = lambda a: a.rearrange("p m a b -> p m (a b)")
                    link(nc.vector.tensor_tensor(flat(CM2), flat(CM2), kc(K_T8).unsqueeze(1).broadcast_to([P, NT, NG * NG]), ALU.mult))
                    link(nc.vector.tensor_tensor(CMP, CMP, CM2, ALU.add))
                    link(nc.vector.tensor_reduce(GK, CMP, AX.X, ALU.add))
                    link(nc.vector.tensor_scalar(GK, GK, float(TOPG), None, ALU.is_lt))
                    g4 = lambda a: a.rearrange("p m (g e) -> p (m g) e", g=NG)
                    gk = GK.rearrange("p m g -> p (m g)").unsqueeze(2).broadcast_to([P, NT * NG, 8])
                    link(nc.vector.tensor_tensor(g4(SM), g4(SE), gk, ALU.mult))
                    link(nc.vector.tensor_scalar(GK, GK, -NEG_BIG, NEG_BIG, ALU.mult, ALU.add))
                    link(nc.vector.tensor_tensor(g4(SM), g4(SM), gk, ALU.add))
                    for m in range(NT):
                        ins = nc.vector.max(T8[:, m, :], SM[:, m, :])
                    link(ins)
                    for m in range(NT):
                        ins = nc.vector.match_replace(MK[:, m, :], T8[:, m, :], SM[:, m, :], -3e38)
                    link(ins)
                    link(nc.vector.tensor_tensor(MK, MK, SM, ALU.not_equal))
                    nc.vector.tensor_tensor(WW, SG, MK, ALU.mult).then_inc(mask_ready, 1)
                    dve.wait_ge(mask_ready, 1)
                    link(nc.vector.tensor_reduce(WSUM, WW, AX.X, ALU.add))
                    link(nc.vector.reciprocal(WSUM, WSUM))
                    link(nc.vector.tensor_tensor(WW, WW, WSUM.unsqueeze(2).broadcast_to([P, NT, NE]), ALU.mult))
                    link(nc.vector.tensor_scalar(WW, WW, ROUTED_SCALE, None, ALU.mult))
                elif st == "table":
                    dve.wait_ge(pos_ready, 1)
                    link(nc.vector.tensor_copy(CNT, PS[:, 7, 0:NE]))
                    link(nc.vector.tensor_scalar(NEX, CNT, 0.0, None, ALU.is_gt))
                    for lim in range(P, T, P):
                        link(nc.vector.tensor_scalar(TMP, CNT, float(lim), None, ALU.is_gt))
                        link(nc.vector.tensor_tensor(NEX, NEX, TMP, ALU.add))
                    link(nc.vector.tensor_tensor_scan(END, ones[:, 0:NE], NEX, 0.0, ALU.mult, ALU.add))
                    link(nc.vector.tensor_tensor(STA, END, NEX, ALU.subtract))
                    link(nc.vector.scalar_tensor_tensor(SE, PS[:, 6, 0:NT * NE].rearrange("p (m e) -> p m e", m=NT), 1.0, MK,
                                                        ALU.add, ALU.mult))
                    link(nc.vector.tensor_scalar(TMP, STA, float(P), -1.0, ALU.mult, ALU.add))
                    link(nc.vector.tensor_tensor(SE, SE, TMP.unsqueeze(1).broadcast_to([P, NT, NE]), ALU.add))
                    rcol = kc(K_COL)[:, 0:1]
                    link(nc.vector.tensor_scalar(EON, STA, rcol, None, ALU.is_le))
                    link(nc.vector.tensor_scalar(TMP, END, rcol, None, ALU.is_gt))
                    link(nc.vector.tensor_tensor(EON, EON, TMP, ALU.mult))
                    link(nc.vector.tensor_tensor(TMP, EON, kc(K_R128)[:, 0:NE], ALU.mult))
                    nc.vector.tensor_reduce(NCNT, TMP, AX.X, ALU.add).then_inc(tab_ready, 1)
                    dve.wait_ge(tab_ready, 1)
                    dve.wait_ge(pr_ready, 1)
                    for m in range(NT):
                        link(nc.vector.scalar_tensor_tensor(POSR[:, m, :], kc(K_R128), -float(P), PS[:, 2, m * P:(m + 1) * P],
                                                            ALU.mult, ALU.add))
                    link(nc.vector.tensor_copy(ROW[0:1, RTAB:RTAB + 1], END[0:1, NE - 1:NE]))
                    nc.vector.tensor_copy(ROW[0:1, 0:RTAB], PS[0:1, 7, 128:256]).then_inc(row_done, 1)
                    for b in range(2):
                        ins = nc.vector.tensor_copy(RHS[:, b, :, :], kc(K_TOK).rearrange("p (m c) -> p m c", m=NT))
                    link(ins)
                    dve.wait_ge(comb_done, 1)
                    for r in range(AHEAD):
                        prep(r, r)
                elif st == "shared":
                    m = ev[1]
                    dve.wait_ge(ss_done, m + 1)
                    nc.vector.tensor_tensor(HID[:, m % 2, :], HS[:, m % 2, :], PS[:, 4 + m % 2, DE:2 * DE], ALU.mult).then_inc(sh_hid, 1)

            def hidden(r, b):
                dve.wait_ge(silu_done, r + 1)
                nc.vector.tensor_tensor(HID[:, b, :], HS[:, b, :], PS[:, 2 + b, DE:2 * DE], ALU.mult).then_inc(hid_done, 1)

            prep(AHEAD, AHEAD)
            hidden(0, 0)
            rounds = dve.value_load(round_count(dve), min_val=1, max_val=ROUNDS)
            with dve.Fori(0, PASSES) as pas:
                for p in range(BODY):
                    i = pas * BODY + (1 + p)
                    with dve.If(i <= rounds):
                        prep(i + AHEAD, (1 + p + AHEAD) % BODY)
                        dve.wait_ge(ht_ready, i)
                        hidden(i, (1 + p) % 2)
                        dve.wait_ge(dn_ready, i)
                        dve.wait_ge(added, i)
                        nc.vector.tensor_scalar(YS[:, p % 2, :].rearrange("p (a n) -> p a n", a=2), PS[:, 6:8, :],
                                                WC[:, p:p + 1], None, ALU.mult).then_inc(ys_done, 1)
            dve.wait_ge(y_back, 16)
            for m in range(NT):
                g2 = GBC[:, 1, min(m, 1), :]
                link(nc.vector.tensor_tensor(YF[:, m, :], YF[:, m, :], g2, ALU.mult))
                nc.vector.tensor_tensor(YF[:, m, :], YF[:, m, :], XH[:, m, :], ALU.add).then_inc(h2_done, 1)
            dve.wait_ge(ssq2, 2 * NT)
            nc.vector.tensor_scalar(small[:, 4:4 + NT], small[:, 0:NT], 1.0 / D, EPS, ALU.mult, ALU.add).then_inc(ms2, 1)
            dve.wait_ge(ms2, 2)
            dve.wait_ge(root2, 2)
            rsqrt_fix(small[:, 4:4 + NT], small[:, 8:8 + NT], small[:, 12:12 + NT], small[:, 24:24 + NT])
            for m in range(NT):
                nc.vector.scalar_tensor_tensor(YN[:, m, :], YF[:, m, :], small[:, 12 + m:13 + m], FG,
                                               ALU.mult, ALU.mult).then_inc(fin_done, 1)

        @block.tensor
        def _(pe):
            mm = nc.tensor.matmul

            def product(out, lhs, rhs, n):
                for k in range(n):
                    last = mm(out, lhs(k), rhs(k), start=(k == 0), stop=(k == n - 1))
                return last

            for ev in SCHEDULE:
                st = ev[0]
                if st == "norm1":
                    pass
                elif st == "unit":
                    n = ev[1]
                    name, c, j = UNITS[n]
                    if n >= 2:
                        pe.wait_ge(unit_taken, n - 1)
                    bank = n % 2
                    if name == "ada":
                        if c == 0:
                            pe.wait_ge(csil_ready, 1)
                        arrived(pe, ("ada", c))
                        w = slot(("ada", c)).rearrange("p (k n) -> p k n", k=KD)
                        product(PS[0:2, bank, :], lambda k: csil[:, k, :], lambda k: w[:, k, :], KD).then_inc(unit_ready, 1)
                    else:
                        tok = name in TOK_CHUNKS
                        if j == 0:
                            arrived(pe, ("in", c))
                            if c == 0:
                                pe.wait_ge(n_ready, KD)
                        w = slot(("in", c)).rearrange("p (k n) -> p k n", k=KD)
                        if tok:
                            product(PS[:, bank, :], lambda k: nT[:, k, j * P:(j + 1) * P], lambda k: w[:, k, :], KD).then_inc(unit_ready, 1)
                        else:
                            product(PS[:, bank, 0:T], lambda k: w[:, k, j * P:(j + 1) * P], lambda k: nT[:, k, :], KD).then_inc(unit_ready, 1)
                elif st == "mod1":
                    pe.wait_ge(unit_taken, 4)
                    pe.wait_ge(in_small, 16)
                    for s in range(2):
                        for k in range(KD):
                            last = mm(PS[:, 7, (s * KD + k) * 2:(s * KD + k) * 2 + 2], ADA[0:2, s * D + k:(s + 1) * D:KD],
                                      ident[0:2, 0:2], start=True, stop=True)
                    last.then_inc(modt_ready, 1)
                    pe.wait_ge(xn_ready, NT)
                    for k in range(KD):
                        if k >= 4:
                            pe.wait_ge(n_ready, k - 3)
                        for m in range(NT):
                            last = nc.tensor.transpose(PS[:, 2 + k % 4, m * P:(m + 1) * P], XN[:, m, k:D:KD], ident)
                        last.then_inc(xnt_ready, 1)
                elif st == "cache":
                    pe.wait_ge(in_cache, 32)
                    for j in range(4):
                        last = nc.tensor.transpose(PS[:, 4, j * P:(j + 1) * P], CK[:, j * P:(j + 1) * P], ident)
                    last.then_inc(ck_t, 1)
                    pe.wait_ge(unit_taken, AFTER["k"])
                    for j in range(4):
                        last = nc.tensor.transpose(PS[:, 5, j * P:(j + 1) * P], KT[:, j, 0:CTX], ident)
                    last.then_inc(ck_t, 1)
                elif st == "scores":
                    h = ev[1]
                    o, j = 64 * (h % 2), h // 2
                    pe.wait_ge(unit_taken, AFTER["v"])
                    pe.wait_ge(ck_taken, 2)
                    for u in range(3):
                        i = 3 * h + u
                        if i >= 2:
                            pe.wait_ge(s_taken, i - 1)
                        bank = 2 + i % 2
                        if u < 2:
                            q = Q[o:o + DH, j, CTX + u * P:CTX + (u + 1) * P]
                            mm(PS[:, bank, 0:2 * P], q, KT[o:o + DH, j, CTX:T], start=True, stop=True)
                            mm(PS[:, bank, 2 * P:3 * P], q, CKT[o:o + DH, j, :], start=True, stop=True).then_inc(s_ready, 1)
                        else:
                            mm(PS[:, bank, 0:P], Q[o:o + DH, j, 0:CTX], KT[o:o + DH, j, 0:CTX], start=True, stop=True).then_inc(s_ready, 1)
                elif st == "values":
                    h = ev[1]
                    o = 64 * (h % 2)
                    for u in range(3):
                        i = 3 * h + u
                        pe.wait_ge(prob_ready, i + 1)
                        if i > 0:
                            pe.wait_ge(pt_taken, i)
                        nk = 3 if u < 2 else 1
                        for k in range(nk):
                            last = nc.tensor.transpose(PS[:, 4, k * P:(k + 1) * P], PR[:, u, k * P:(k + 1) * P], ident)
                        last.then_inc(pt_ready, 1)
                    if h > 0:
                        pe.wait_ge(pv_taken, h)
                    pe.wait_ge(pt_taken, 3 * h + 3)
                    vs = [V[:, 1, h * DH:(h + 1) * DH], V[:, 2, h * DH:(h + 1) * DH], CV[:, h * DH:(h + 1) * DH]]
                    product(PS[o:o + DH, 5, 0:2 * P], lambda k: vs[k], lambda k: PT[:, k, :], 3)
                    mm(PS[o:o + DH, 5, 2 * P:3 * P], V[:, 0, h * DH:(h + 1) * DH], PTC, start=True, stop=True).then_inc(pv_ready, 1)
                elif st == "level":
                    i = ev[1]
                    pe.wait_ge(qk_done, i + 1)
                    if i > 0:
                        pe.wait_ge(lev_taken, i)
                    for hh in range(2):
                        for m in range(NT):
                            s = slice(hh * T + m * P, hh * T + (m + 1) * P)
                            last = mm(PS[:, 6 + hh, m * P:(m + 1) * P], KX[:, s], QX[:, s], start=True, stop=True)
                    last.then_inc(lev_ready, 1)
                elif st == "carry_t":
                    for c in range(4):
                        pe.wait_ge(kh_done, c + 1)
                        if c >= 2:
                            pe.wait_ge(kht_taken, c - 1)
                        for h in range(HC):
                            last = nc.tensor.transpose(PS[:, 4 + c % 2, h * P:(h + 1) * P], KH[:, c, h, :], ident)
                        last.then_inc(kht_ready, 1)
                elif st == "carry_products":
                    pe.wait_ge(lev_taken, 16)
                    pe.wait_ge(unit_taken, AFTER["ic"])
                    for c, m in enumerate((0, 0, 1, 2)):
                        pe.wait_ge(kht_taken, c + 1)
                        if c == 2:
                            pe.wait_ge(st_done, 1)
                        if c == 3:
                            pe.wait_ge(st_done, 2)
                        for h in range(HC):
                            last = mm(PS[:, 6 + c % 2, h * P:(h + 1) * P], KHT[:, c, h, :], IC[:, m, h * P:(h + 1) * P], start=True, stop=True)
                        last.then_inc(kv_ready, 1)
                elif st == "hout":
                    m = ev[1]
                    if m == 0:
                        pe.wait_ge(st_done, 3)
                    else:
                        pe.wait_ge(ho_taken, m)
                    for h in range(HC):
                        out = PS[:, 6, h * P:(h + 1) * P]
                        v = IC[:, m, h * P:(h + 1) * P]
                        last = mm(out, AT_[:, h, m, :], v, start=True, stop=(m == 0))
                        if m > 0:
                            sf = ST if m == 1 else ST2
                            sb_ = ST if m == 2 else ST2
                            mm(out, EB[:, 0, h, (m - 1) * P:m * P], sf[:, 0, h, :], start=False, stop=False)
                            last = mm(out, EB[:, 1, h, (m - 1) * P:m * P], sb_[:, 1, h, :], start=False, stop=True)
                    last.then_inc(ho_ready, 1)
                elif st == "hout_t":
                    m = ev[1]
                    pe.wait_ge(ho_norm, m + 1)
                    if m > 0:
                        pe.wait_ge(hot_taken, m)
                    for h in range(HC):
                        last = nc.tensor.transpose(PS[:, 7, h * P:(h + 1) * P], OR[:, h * P:(h + 1) * P], ident)
                    last.then_inc(hot_ready, 1)
                elif st == "mod2":
                    pe.wait_ge(unit_taken, len(UNITS))
                    pe.wait_ge(hot_taken, NT)
                    for s in range(2):
                        for k in range(KD):
                            last = mm(PS[:, 7, (s * KD + k) * 2:(s * KD + k) * 2 + 2], Zrows[:, s * D + k:(s + 1) * D:KD],
                                      ident[0:2, 0:2], start=True, stop=True)
                    last.then_inc(modt_ready, 1)
                    pe.wait_ge(gr_ready, 1)
                    for i in range(8):
                        g, v, hf = i // 4, i // 2 % 2, i % 2
                        if i >= 4:
                            pe.wait_ge(gb_taken, i - 3)
                        mm(PS[:, 2 + i % 4, :], sel[0:2, v, :], GR[0:2, g * D + hf * 512:g * D + (hf + 1) * 512],
                           start=True, stop=True).then_inc(gb_ready, 1)
                elif st == "branches":
                    pe.wait_ge(gb_taken, 8)
                    for i in range(24):
                        j, br = i // 3, i % 3
                        if i < 3:
                            arrived(pe, ("br", br))
                        if i >= 6:
                            pe.wait_ge(br_taken, i - 5)
                        w = slot(("br", br)).rearrange("p (k n) -> p k n", k=4)
                        src = (OA, GB, OCT)[br]
                        product(PS[:, i % 6, 0:T], lambda k: w[:, k, j * P:(j + 1) * P], lambda k: src[:, k, :], 4).then_inc(br_ready, 1)
                elif st == "wout":
                    pe.wait_ge(mix_done, 8)
                    for i in range(2 * NT):
                        m, hf = i // 2, i % 2
                        arrived(pe, ("out", hf))
                        if i >= 2:
                            pe.wait_ge(wo_taken, i - 1)
                        w = slot(("out", hf)).rearrange("p (k n) -> p k n", k=KD)
                        product(PS[:, 6 + i % 2, :], lambda k: G[:, k, m * P:(m + 1) * P], lambda k: w[:, k, :], KD).then_inc(wo_ready, 1)
                elif st == "norm2":
                    pe.wait_ge(xn2, NT)
                    for k in range(KD):
                        if k >= 4:
                            pe.wait_ge(n2_ready, k - 3)
                        for m in range(NT):
                            last = nc.tensor.transpose(PS[:, 2 + k % 4, m * P:(m + 1) * P], XN2[:, m, k:D:KD], ident)
                        last.then_inc(xnt2, 1)
                    pe.wait_ge(n2_ready, KD)
                    for i in range(2 * NT):
                        m, hf = i // 2, i % 2
                        if i >= 2:
                            pe.wait_ge(n2_rowed, i - 1)
                        for k in range(4):
                            last = nc.tensor.transpose(PS[:, 6 + i % 2, k * P:(k + 1) * P], nT[:, 4 * hf + k, m * P:(m + 1) * P], ident)
                        last.then_inc(n2t_ready, 1)
                elif st == "router":
                    pe.wait_ge(fin_loaded, 48)
                    pe.wait_ge(n2_rowed, 2 * NT)
                    for m in range(NT):
                        last = product(PS[:, 6, m * NE:(m + 1) * NE], lambda k: nT[:, k, m * P:(m + 1) * P], lambda k: WR[:, k, :], KD)
                    last.then_inc(rt_ready, 1)
                elif st == "table":
                    pe.wait_ge(mask_ready, 1)
                    for m in range(NT):
                        lhs = [ones] * m + [kc(K_TRI)]
                        last = product(PS[:, 6, m * NE:(m + 1) * NE], lambda k: lhs[k], lambda k: MK[:, k, :], m + 1)
                    product(PS[:, 7, 0:NE], lambda k: ones, lambda k: MK[:, k, :], NT).then_inc(pos_ready, 1)
                    pe.wait_ge(tab_ready, 1)
                    nc.tensor.transpose(PS[0:NE, 6, 0:P], EON, ident)
                    for m in range(NT):
                        nc.tensor.transpose(PS[0:NE, 6, (m + 1) * P:(m + 2) * P], SE[:, m, :], ident)
                        nc.tensor.transpose(PS[0:NE, 7, m * P:(m + 1) * P], WW[:, m, :], ident).then_inc(te_ready, 1) if m == NT - 1 else \
                            nc.tensor.transpose(PS[0:NE, 7, m * P:(m + 1) * P], WW[:, m, :], ident)
                    pe.wait_ge(te_taken, 1)
                    mm(PS[0:1, 7, P:2 * P], NCNT, ident, start=True, stop=True)
                    for m in range(NT):
                        mm(PS[:, 2, m * P:(m + 1) * P], TE[0:NE, 1 + m, :], TE[0:NE, 0, :], start=True, stop=True)
                        last = mm(PS[:, 3, m * P:(m + 1) * P], TE[0:NE, 4 + m, :], TE[0:NE, 0, :], start=True, stop=True)
                    last.then_inc(pr_ready, 1)
                elif st == "shared":
                    m = ev[1]
                    if m == 0:
                        pe.wait_ge(sh_loaded, 48)
                    wg = slot(("sh", 0)).rearrange("p (k n) -> p k n", k=KD)
                    wd = slot(("shd", 0))[:, 0:2 * D].rearrange("p (k n) -> p k n", k=2)
                    if m >= 2:
                        pe.wait_ge(sh_hid, m - 1)
                    product(PS[:, 4 + m % 2, :], lambda k: nT[:, k, m * P:(m + 1) * P], lambda k: wg[:, k, :], KD).then_inc(sg_ready, 1)
                    pe.wait_ge(sh_hid, m + 1)
                    for k in range(2):
                        last = nc.tensor.transpose(PS[:, 0, k * P:(k + 1) * P], HID[:, m % 2, k * P:(k + 1) * P], ident)
                    last.then_inc(sht_ready, 1)
                    pe.wait_ge(sht_taken, m + 1)
                    if m > 0:
                        pe.wait_ge(sho_done, m)
                    for hf in range(2):
                        last = product(PS[:, 1 + hf, :], lambda k: HT[:, m % 2, k, :], lambda k: wd[:, k, hf * 512:(hf + 1) * 512], 2)
                    last.then_inc(shd_ready, 1)

            def index(r, b):
                pe.wait_ge(oh_done, r + 1)
                if not isinstance(r, int) or r > 0:
                    pe.wait_ge(idx_done, r)
                product(PS[:, 4, 0:3], lambda m: OH[:, b, m, :], lambda m: RHS[:, b, m, :], NT).then_inc(ix_ready, 1)

            def transposes(turn, b):
                pe.wait_ge(gathered[b], 16 * turn)
                for k in range(KD):
                    last = nc.tensor.transpose(PS[:, k // 4, k % 4 * P:(k % 4 + 1) * P], XG[:, b, k:D:KD], ident)
                last.then_inc(xg_t, 1)

            def gate_up(r, turn, p, ks):
                b, q = p % 2, p % WS
                if 0 in ks:
                    pe.wait_ge(gu_loaded[q], 32 * turn)
                    pe.wait_ge(xt_done, r + 1)
                for k in ks:
                    last = mm(PS[:, 2 + b, :], XT[:, b, k, :], GU_W[q][:, k, :], start=(k == 0), stop=(k == KD - 1))
                if KD - 1 in ks:
                    last.then_inc(gu_ready, 1)

            pe.wait_ge(sho_done, NT)
            for r in range(AHEAD):
                index(r, r % 2)
            transposes(1, 0)
            pe.wait_ge(xt_done, 1)
            transposes(1, 1)
            index(AHEAD, AHEAD % 2)
            gate_up(0, 1, 0, range(KD))
            rounds = pe.value_load(round_count(pe), min_val=1, max_val=ROUNDS)
            with pe.Fori(0, PASSES) as pas:
                for p in range(BODY):
                    i = pas * BODY + (1 + p)
                    with pe.If(i <= rounds):
                        pe.wait_ge(xt_done, i + 1)
                        transposes(pas * (BODY // XGS) + (2 + p) // XGS + 1, (2 + p) % XGS)
                        pe.wait_ge(hid_done, i)
                        turn = pas * (BODY // WS) + (1 + p) // WS + 1
                        gate_up(i, turn, 1 + p, range(0, 4))
                        pe.wait_ge(hid_done, i + 1)
                        for k in range(2):
                            last = nc.tensor.transpose(PS[:, 5, k * P:(k + 1) * P], HID[:, p % 2, k * P:(k + 1) * P], ident)
                        last.then_inc(ht_ready, 1)
                        index(i + AHEAD, (1 + p + AHEAD) % 2)
                        gate_up(i, turn, 1 + p, range(4, KD))
                        q = p % WS
                        pe.wait_ge(dn_loaded[q], 16 * (pas * (BODY // WS) + p // WS + 1))
                        pe.wait_ge(ht_done, i)
                        pe.wait_ge(ys_done, i)
                        for hf in range(2):
                            last = product(PS[:, 6 + hf, :], lambda k: HT[:, p % 2, k, :],
                                           lambda k: DN_W[q][:, k, hf * 512:(hf + 1) * 512], 2)
                        last.then_inc(dn_ready, 1)


_OUTS = [("y", (T, D)), ("new_k", (P, 512)), ("new_v", (P, 512)), ("new_state", (2, HC, P, P))]


def kernel(**inputs):
    import concourse.bacc as _bacc
    from concourse.bass_utils import run_bass_kernel_spmd as _run

    a = {k: np.ascontiguousarray(v) for k, v in inputs.items()}
    pk = lambda v: v.reshape(P, KD)
    hp = lambda v: v.reshape(-1, P).T
    b_ada = a["b_ada"][0].reshape(6, D)
    cols = np.concatenate(
        [pk(a["norm1_g"][0]), pk(a["norm2_g"][0]), pk(a["c_ctx"]), pk(a["c"][0])]
        + [pk(b_ada[i]) for i in (0, 1, 3, 4)]
        + [hp(a["lb_fwd"][0]), hp(a["lb_bwd"][0]), hp(a["w_conv"][0]), hp(a["hgrn_norm_g"][0])], 1)
    w_ada = a["w_ada"][0]
    arrays = {
        "x": np.concatenate([a["x_prompt"][0], a["x_sample"][0]], 0),
        "consts": shape_constants(),
        "cols": cols,
        "b_gate": np.tile(np.concatenate([b_ada[2], b_ada[5]])[None], (2, 1)),
        "w_ada": w_ada,
        "w_in": a["w_in"][0],
        "w_br": np.concatenate([a["w_br_a"], a["w_br_b"], a["w_br_c"]], 0),
        "w_out": a["w_out"][0],
        "rpb": a["rpb"][0],
        "cache_k": a["cache_k"].reshape(P, 512),
        "cache_v": a["cache_v"].reshape(P, 512),
        "state": a["state_hgrn"][0, 0],
        "w_router": a["w_router"][0],
        "b_router": a["b_router"][0],
        "w_sh_gate": a["w_sh_gate"][0],
        "w_sh_up": a["w_sh_up"][0],
        "w_sh_down": a["w_sh_down"][0],
        "w_gate": a["w_gate"][0],
        "w_up": a["w_up"][0],
        "w_down": a["w_down"][0],
        "final_g": a["final_norm_g"],
    }
    arrays = {k: np.ascontiguousarray(v) for k, v in arrays.items()}
    nc = _bacc.Bacc("TRN2", target_bir_lowering=False, num_devices=1)
    args = [nc.dram_tensor(f"in_{k}", v.shape, mybir.dt.from_np(v.dtype), kind="ExternalInput").ap() for k, v in arrays.items()]
    outs = [nc.dram_tensor(f"out_{k}", shape, F32, kind="ExternalOutput").ap() for k, shape in _OUTS]
    trunk(nc, *args, *outs)
    r = _run(nc, [{f"in_{k}": v for k, v in arrays.items()}], core_ids=[0]).results[0]
    y = r["out_y"]
    return (y[:P].reshape(1, P, D), y[P:].reshape(1, T - P, D),
            r["out_new_k"].reshape(1, 1, P, NH, DH), r["out_new_v"].reshape(1, 1, P, NH, DH),
            r["out_new_state"].reshape(1, 1, 2, HC, P, P))
```

```python
from contextlib import ExitStack

import numpy as np

import concourse.bass as bass
from concourse import mybir

F32 = mybir.dt.float32
F32R = mybir.dt.float32r
I32 = mybir.dt.int32
U32 = mybir.dt.uint32
ALU = mybir.AluOpType
ACT = mybir.ActivationFunctionType
AX = mybir.AxisListType

P = 128
D = 1024
KD = D // P
NT = 3
T = NT * P
CTX = P
GRID_W = 64
NH, DH = 8, 64
HC = 4
WCH = 512
NE, TOPK, NG, TOPG = 64, 8, 8, 4
DE = 256
ROUTED_SCALE = 2.5
EPS = 1e-6
NEG_BIG = -1e30
LOG_FLOOR = 1e-30
LEVELS = (2, 4, 8, 16, 32, 64, 128)
ROUNDS = NE + (T * TOPK - NE) // P
RTAB = P
BODY = 12
PASSES = (ROUNDS + BODY - 1) // BODY
WS, XGS, AHEAD = 3, 4, 4

K_ID, K_MASK, K_LEV, K_SCAN, K_SEL, K_TRI, K_ONE, K_R128, K_TOK, K_COL, K_T8, K_END = range(12)
K_W = [P, GRID_W, 7 * P, T, 2 * P, P, P, P, NT * 3, 2, NG * NG, 0]
K_AT = [sum(K_W[:i]) for i in range(12)]
C_N1, C_N2, C_C, C_ADA, C_LB, C_CONV, C_HG = range(7)
C_W = [KD, KD, 2 * KD, 4 * KD, 2 * HC, 12, HC]
C_AT = [sum(C_W[:i]) for i in range(8)]


def shape_constants():
    k = np.zeros((P, K_AT[K_END]), np.float32)
    p = np.arange(P)
    put = lambda i, a: k.__setitem__((slice(None), slice(K_AT[i], K_AT[i] + K_W[i])), a)
    put(K_ID, np.eye(P))
    qc = (GRID_W - 1 - p % GRID_W)[:, None]
    kc = np.arange(GRID_W)[None, :]
    start = np.clip(qc - 8, 0, GRID_W - 16)
    put(K_MASK, np.where((kc >= start) & (kc < start + 16), 0.0, NEG_BIG))
    s, t = p[:, None], p[None, :]
    put(K_LEV, np.concatenate([((s // L == t // L) & ((s % L < L // 2) != (t % L < L // 2))) for L in LEVELS], 1))
    put(K_SCAN, np.tile((np.arange(T) % P != 0).astype(np.float32), (P, 1)))
    sel = np.zeros((P, 2, P)); sel[0, 0] = 1; sel[1, 1] = 1
    put(K_SEL, sel.reshape(P, -1))
    put(K_TRI, (s < t))
    put(K_ONE, np.ones((P, P)))
    put(K_R128, np.tile(p[None, :].astype(np.float32), (P, 1)))
    tok = np.stack([np.stack([p + P * m, np.ones(P), np.zeros(P)], 1) for m in range(NT)], 1)
    put(K_TOK, tok.reshape(P, -1))
    put(K_COL, np.stack([p, p + T], 1))
    g = np.arange(NG)
    put(K_T8, np.tile((g[None, :] < g[:, None]).astype(np.float32).reshape(1, -1), (P, 1)))
    return k


STREAM = ([("ada", n) for n in range(4)]
          + [("in", n) for n in range(17)]
          + [("ada", n) for n in range(4, 12)]
          + [("br", n) for n in range(3)]
          + [("out", n) for n in range(2)]
          + [("sh", 0), ("shd", 0)])
SLOT_OF = {key: n for n, key in enumerate(STREAM)}
NSLOT = 3
IN_CHUNKS = ["v", "ic", "q", "k", "u", "gb", "gc", "qc", "zf", "zb", "oc"] + [f"g{n}" for n in range(6)]
TOK_CHUNKS = ("v", "ic")
SPLIT = ("q", "k", "u", "gb", "gc", "qc", "zf", "zb", "oc")


def projection_units():
    units = []
    for n in range(4):
        units.append(("ada", n, 0))
    for c, name in enumerate(IN_CHUNKS):
        for j in range(NT if name in TOK_CHUNKS else 4):
            units.append((name, c, j))
    for n in range(4, 12):
        units.append(("ada", n, 0))
    return units


UNITS = projection_units()
AFTER = {}
for _n, (_name, _c, _j) in enumerate(UNITS):
    AFTER[("ada", _c) if _name == "ada" else _name] = _n + 1


SPLIT_G = list(range(AFTER["oc"], AFTER["oc"] + 19))


def unit_stages(n):
    name, c, j = UNITS[n]
    s = [("unit", n)]
    if n + 1 == AFTER["v"]:
        s.append(("n_high",))
    if n + 1 == AFTER["ic"]:
        s.append(("n_low",))
    if n + 3 == AFTER["oc"]:
        s.append(("n_move",))
    if n + 2 in SPLIT_G:
        s.append(("split_g", n + 2))
    if n == SPLIT_G[-1]:
        s.append(("n_back",))
    nxt = IN_CHUNKS[c + 1] if name != "ada" and c + 1 < len(IN_CHUNKS) else None
    if nxt in SPLIT:
        if name in TOK_CHUNKS and j < 2:
            s.append(("split", nxt, j))
        elif name not in TOK_CHUNKS and j % 2:
            s.append(("split", nxt, j // 2))
    return s


def schedule():
    s = [("csilu",)]
    att = 0
    fill = []
    for n, (name, c, j) in enumerate(UNITS):
        if n + 1 > AFTER["zb"]:
            fill.append(unit_stages(n))
            continue
        s += unit_stages(n)
        if n == 1:
            s.append(("norm1",))
        if n + 1 == AFTER[("ada", 3)]:
            s.append(("mod1",))
        if n + 1 > AFTER["k"] and att <= NH and j % 2 == 0:
            if att > 0:
                s.append(("values", att - 1))
            if att < NH:
                s.append(("scores", att))
            att += 1
        if name == "qc":
            s.append(("conv", j))
        if n + 1 == AFTER["k"]:
            s.append(("cache",))
    stages = [(("gates",), 3), (("decays",), 1), (("sums",), 3), (("ops", 0), 1)]
    for i in range(16):
        stages += [(("level", i), 0), (("ops", i + 1) if i < 15 else ("carry",), 1 if i < 15 else 2)]
    stages += [(("carry_t",), 2), (("carry_products",), 2), (("hout", 0), 1), (("hout_t", 0), 1), (("hout", 1), 1),
               (("hout_t", 1), 1), (("hout", 2), 1), (("hout_t", 2), 0)]
    for stage, n in stages:
        s += [stage] + sum(fill[:n], [])
        fill = fill[n:]
    late = [("late_act", b) for b in range(3)]
    while fill or late:
        s += late[:1] + sum(fill[:1], [])
        late, fill = late[1:], fill[1:]
    s += [("branches",), ("mod2",), ("gate1",), ("wout", 0, 0), ("wout", 0, 1), ("norm2", 0), ("wout", 1, 0),
          ("wout", 1, 1), ("norm2", 1), ("norm_t", 0), ("gate2",), ("wout", 2, 0), ("norm_t", 1), ("wout", 2, 1),
          ("norm2", 2), ("rows", 0), ("rows", 1), ("sh_up", 0), ("norm_t", 2), ("router",), ("rows", 2), ("sh_up", 1),
          ("counts",), ("sh_down", 0), ("sh_down", 1), ("table_t",), ("table",), ("index", 0), ("sh_up", 2),
          ("index", 1), ("sh_down", 2), ("index", 2), ("index", 3)]
    return s


SCHEDULE = schedule()
assert [x for x in SCHEDULE if x[0] == "values"][-1][1] == NH - 1


def trunk(nc, x, consts, cols, b_gate, w_ada, w_in, w_br, w_out, rpb, cache_k, cache_v, state, w_router, b_router,
          w_sh_gate, w_sh_up, w_sh_down, w_gate, w_up, w_down, final_g, y, new_k, new_v, new_state):
    n2_rows = nc.dram_tensor("n2_rows", (4 * P, D), F32, kind="Internal").ap()
    y_rows = nc.dram_tensor("y_rows", (4 * P, D), F32, kind="Internal").ap()
    with ExitStack() as ctx:
        def sb(name, shape, dt=F32):
            return ctx.enter_context(nc.sbuf_tensor(name, shape, dt))

        def sem(name):
            return ctx.enter_context(nc.semaphore(name))

        PS = ctx.enter_context(nc.psum_tensor("PS", [P, 8, 512], F32))

        K = sb("K", [P, K_AT[K_END]])
        C = sb("C", [P, C_AT[7]])
        kc = lambda i: K[:, K_AT[i]:K_AT[i] + K_W[i]]
        cc = lambda i: C[:, C_AT[i]:C_AT[i] + C_W[i]]
        ident = kc(K_ID)
        levmask = kc(K_LEV).bitcast(U32).rearrange("p (l t) -> p l t", l=7)
        sel = kc(K_SEL).rearrange("p (v t) -> p v t", v=2)
        ones = kc(K_ONE)
        def with_rounded(name, shape, n):
            with nc.sbuf_tensor(name + "_r", [P, n], F32R) as r:
                pass
            return sb(name, shape), r

        nT, nT_r = with_rounded("nT", [P, KD, T], KD * T)
        bigA, bigA_r = with_rounded("bigA", [P, NSLOT * 4096], NSLOT * 4096)
        bigB, bigB_r = with_rounded("bigB", [P, 24608], 12288 + KD * P)
        bigC, bigC_r = with_rounded("bigC", [P, 5760], KD * T + KD * P + 2 * T)
        small = sb("small", [P, 128])
        modc = sb("modc", [P, 4, 2, KD])
        csil = sb("csil", [P, KD, 2])
        bigD = sb("bigD", [P, 3 * 1536])
        ring = bigA[:, :].rearrange("p (s n) -> p s n", s=NSLOT)

        def cut(t, at, shape, names="abcd"):
            n = int(np.prod(shape))
            v = t[:, at:at + n]
            if len(shape) == 1:
                return v
            ax = names[:len(shape)]
            return v.rearrange("p (" + " ".join(ax) + ") -> p " + " ".join(ax), **dict(zip(ax[:-1], shape[:-1])))

        G = cut(bigB, 0, (24, T))
        X = cut(bigB, 0, (NT, D))
        XN = cut(bigB, 3072, (NT, D))
        ADA = bigB[:, 6144:8192]
        NHI = cut(bigB_r, 0, (KD, T))
        NLO = cut(nT_r, 0, (KD, T))
        WHI = cut(bigB_r, 3072, (2, KD, 256))
        WLO = cut(bigA_r, 0, (NSLOT, KD, 512))
        NHI2 = cut(bigC_r, 0, (KD, T))
        GHI = [cut(bigC_r, 3072, (KD, P)), cut(bigB_r, 12288, (KD, P))]
        CK = bigB[:, 8192:8704]
        CKO = bigB[:, 8704:9216]
        ATT = 9216
        Q = cut(bigB, ATT, (4, T))
        KT = cut(bigB, ATT + 1536, (4, T))
        V = cut(bigB, ATT + 3072, (NT, 512))
        E = cut(bigB, ATT, (2, 768))
        QX = bigB[:, ATT + 1536:ATT + 2304]
        KX = bigB[:, ATT + 2304:ATT + 3072]
        KH = cut(bigB, ATT, (4, HC, P))
        KHT = cut(bigB, ATT + 2048, (4, HC, P))
        ST2 = cut(bigB, ATT, (2, HC, P))
        XH = cut(bigB, ATT, (NT, D))
        T1 = bigB[:, ATT + 3072:ATT + 3584]
        FG = bigB[:, ATT + 3584:ATT + 4608]
        UU = cut(bigB, 13824, (4, T))
        AT_ = cut(bigB, 13824, (HC, NT, P))
        OCT = UU
        GB = cut(bigB, 15360, (4, T))
        GC = cut(bigB, 16896, (4, 388))
        ZP = cut(bigB, 18448, (4, 388))
        KEY = cut(bigB, 16896, (2, HC, T))
        BG = bigB[:, 16896:18944]
        QC = cut(bigB, 20000, (HC, T))
        Z = cut(bigB, 21536, (2, HC, T))
        GR = bigB[:, 20000:22048]
        Zrows = bigB[0:2, 22048:24096]
        BIAS = cut(bigC, 0, (2, 2, T))
        CV = bigC[:, 1536:2048]
        CKT = cut(bigC, 2048, (4, P))
        SB = cut(bigC, 2560, (3, T))
        PR = cut(bigC, 3712, (3, T))
        PT = cut(bigC, 4864, (3, 2 * P))
        PTC = bigC[:, 5632:5760]
        EB = cut(bigC, 0, (2, HC, 2 * P))
        STC = cut(bigC, 2048, (2, HC, P))
        OS, OQ, OR = bigC[:, 3072:3584], bigC[:, 3584:4096], bigC[:, 4096:4608]
        ST = cut(bigC, 4608, (2, HC, P))
        GBC = cut(bigC, 0, (2, 2, D))
        IC = cut(bigD, 0, (NT, 512))
        OG = cut(bigD, 1536, (HC, T))
        OA = cut(bigD, 3072, (4, T))
        WSLOT = [bigB[:, 0:6144], bigA[:, 0:6144], bigA[:, 6144:12288]]
        GU_W = [w[:, 0:4096].rearrange("p (k n) -> p k n", k=KD) for w in WSLOT]
        DN_W = [w[:, 4096:6144].rearrange("p (k n) -> p k n", k=2) for w in WSLOT]
        XN2 = cut(bigB, 16896, (NT, D))
        N2 = cut(bigB, 3072, (NT, D))
        XG = cut(bigB, 16896, (XGS, D))
        HID = cut(bigB, 8192, (2, DE))
        HT = cut(bigB, 8704, (2, 2, P))
        SHO = cut(bigB, 13824, (NT, D))
        XT = cut(bigB, 6144, (2, KD, P))
        YS = cut(bigB, 22016, (2, D))
        HS = cut(bigB, 24064, (2, DE))
        WR = cut(bigD, 0, (KD, NE))
        BR = bigD[:, 512:576]
        SG = cut(bigD, 576, (NT, NE))
        SE = cut(bigD, 768, (NT, NE))
        SM = cut(bigD, 960, (NT, NE))
        MK = cut(bigD, 1152, (NT, NE))
        WW = cut(bigD, 1344, (NT, NE))
        M8 = cut(bigD, 1536, (NT, NG, 8))
        CMP = cut(bigD, 1728, (NT, NG, NG))
        CM2 = cut(bigD, 1920, (NT, NG, NG))
        CNT, NEX, END, STA, EON, TMP = (bigD[:, 2112 + 64 * i:2176 + 64 * i] for i in range(6))
        TE = cut(bigD, 2496, (7, P))
        POSR = cut(bigD, 3392, (NT, P))
        COMB = cut(bigD, 3776, (NT, P))
        GS = cut(bigD, 4160, (NT, NG))
        GK = cut(bigD, 4184, (NT, NG))
        T8 = cut(bigD, 4208, (NT, 8))
        WSUM = bigD[:, 4232:4235]
        RHS = sb("RHS", [P, 2, NT, 4], F32R)
        OH = cut(bigC_r, 4096, (2, NT, P))
        COMBL = cut(bigD, 2496, (NT, P))
        WC = bigD[:, 4260:4260 + BODY]
        NCNT = bigD[:, 4272:4273]
        IDX = sb("IDX", [P, BODY], I32)
        ROW = sb("ROW", [1, RTAB + 4], I32)
        YF = cut(bigA, 0, (NT, D))
        YN = cut(bigA, 3072, (NT, D))

        loaded = [sem(f"weights_loaded_{i}") for i in range(NSLOT)]
        in_small = sem("constants_loaded")
        in_cols = sem("small_vectors_loaded")
        in_x = sem("x_loaded")
        in_cache = sem("cache_loaded")
        in_state = sem("state_loaded")
        in_bias = [sem("bias_loaded_0"), sem("bias_loaded_1")]
        bias_masked = sem("bias_masked")
        in_xh = sem("residual_loaded")
        out_done = sem("outputs_written")
        ssq_done = sem("sum_of_squares")
        ssq_of = sem("root_mean_square")
        root_done = sem("root")
        xn_ready = sem("normed_tile")
        xnt_ready = sem("normed_transposed")
        n_ready = sem("modulated")
        unit_ready = sem("unit_ready")
        unit_taken = sem("unit_taken")
        csil_ready = sem("csilu_ready")
        nhi_done = sem("n_high_ready")
        nlo_done = sem("n_low_ready")
        nback_done = sem("n_whole_again")
        nmove_done = sem("n_high_moved")
        ghi_done = sem("gate_w_high_ready")
        glo_done = sem("gate_w_low_ready")
        whi_done = sem("w_high_ready")
        wlo_done = sem("w_low_ready")
        modt_ready = sem("mod_transposed")
        mod_ready = sem("mod_ready")
        ck_t = sem("cache_transposed")
        ck_taken = sem("cache_t_taken")
        s_ready = sem("scores_ready")
        s_taken = sem("scores_taken")
        max_ready = sem("max_ready")
        exp_ready = sem("exp_ready")
        prob_ready = sem("probs_ready")
        pt_ready = sem("probs_transposed")
        pt_taken = sem("probs_t_taken")
        pv_ready = sem("values_ready")
        pv_taken = sem("values_taken")
        conv_done = sem("conv_done")
        sig_done = sem("gate_sigmoids")
        f_done = sem("forget_ready")
        logf_done = sem("logf_ready")
        b_done = sem("decay_sums")
        diff_done = sem("level_diff")
        edec_done = sem("level_decay")
        qk_done = sem("level_operands")
        lev_ready = sem("level_products")
        lev_taken = sem("level_taken")
        at_zero = sem("pairwise_terms_zeroed")
        kh_done = sem("carry_keys")
        kht_ready = sem("carry_keys_t")
        kht_taken = sem("carry_keys_t_taken")
        kv_ready = sem("carry_products")
        st_done = sem("states_done")
        ho_ready = sem("hgrn_out_ready")
        ho_taken = sem("hgrn_out_copied")
        ho_ms = sem("hgrn_mean_square")
        ho_root = sem("hgrn_root")
        ho_norm = sem("hgrn_normed")
        hot_ready = sem("hgrn_out_t")
        hot_taken = sem("hgrn_out_t_taken")
        late_done = sem("late_sigmoids")
        gb_ready = sem("gate_rows_spread")
        gb_taken = sem("gate_rows_taken")
        g2_ready = sem("gate_rows_2_spread")
        g2_taken = sem("gate_rows_2_taken")
        br_ready = sem("branch_products")
        br_taken = sem("branch_taken")
        mix_done = sem("mix_done")
        wo_ready = sem("out_products")
        wo_taken = sem("out_taken")
        dve_order = sem("dve_order")
        prep_order = sem("prep_order")
        act_order = sem("act_order")
        pool_order = sem("pool_order")
        gather_go = sem("gather_may_start")
        added = sem("results_added_through")
        sh_loaded = sem("shared_weights_loaded")
        bg_loaded = sem("gate_bias_loaded")
        gr_ready = sem("gate_rows_ready")
        state_out = sem("states_written")
        cache_out = sem("caches_written")
        fin_loaded = sem("final_weights_loaded")
        ssq2 = sem("sum_of_squares_2")
        ms2 = sem("mean_square_2")
        root2 = sem("root_2")
        xn2 = sem("normed_2")
        xnt2 = sem("normed_transposed_2")
        n2_ready = sem("modulated_2")
        n2t_ready = sem("rows_2_in_psum")
        n2_rowed = sem("rows_2_copied")
        n2_out = sem("rows_2_written")
        rt_ready = sem("router_logits")
        rt_sig = sem("router_sigmoids")
        mask_ready = sem("expert_mask")
        pos_ready = sem("positions_counts")
        tab_ready = sem("round_table_operands")
        te_ready = sem("table_transposed")
        te_taken = sem("table_transposed_taken")
        pr_ready = sem("round_positions")
        comb_done = sem("round_weights_taken")
        row_done = sem("round_row")
        sg_ready = sem("shared_gate_up")
        ss_done = sem("shared_silu")
        sh_hid = sem("shared_hidden")
        sht_ready = sem("shared_hidden_t")
        sht_taken = sem("shared_hidden_t_taken")
        shd_ready = sem("shared_down")
        sho_done = sem("shared_out")
        y_init = sem("y_rows_initialised")
        gu_loaded = [sem(f"gate_up_loaded_{i}") for i in range(WS)]
        dn_loaded = [sem(f"down_loaded_{i}") for i in range(WS)]
        oh_done = sem("one_hots")
        ix_ready = sem("index_products")
        idx_done = sem("indices")
        gathered = [sem(f"gathered_{i}") for i in range(XGS)]
        xg_t = sem("gathered_t")
        xt_done = sem("gathered_t_taken")
        gu_ready = sem("gate_up_products")
        silu_done = sem("silu")
        hid_done = sem("hidden")
        ht_ready = sem("hidden_t")
        ht_done = sem("hidden_t_taken")
        dn_ready = sem("down_products")
        ys_done = sem("results_weighted")
        scat = sem("results_added")
        y_back = [sem(f"sums_loaded_{m}") for m in range(NT)]
        ssq3 = sem("sum_of_squares_3")
        ms3 = sem("mean_square_3")
        root3 = sem("root_3")
        h2_done = sem("residual_2")
        fin_done = sem("final_normed")

        block = ctx.enter_context(nc.Block())

        def arrived(eng, key):
            n = SLOT_OF[key]
            eng.wait_ge(loaded[n % NSLOT], 16 * (n // NSLOT + 1))

        def slot(key):
            return ring[:, SLOT_OF[key] % NSLOT, :]

        def free_after(eng, key):
            src, i = key
            if src == "ada":
                eng.wait_ge(unit_ready, AFTER[("ada", i)])
            elif src == "in":
                eng.wait_ge(unit_ready, AFTER[IN_CHUNKS[i]])
            elif src == "br":
                eng.wait_ge(br_ready, KD * (i + 1))
            elif src == "out":
                eng.wait_ge(wo_ready, 2 * NT)

        def half_of(name, half):
            c = IN_CHUNKS.index(name)
            w = slot(("in", c)).rearrange("p (k n) -> p k n", k=KD)
            cols = slice(half * 256, (half + 1) * 256)
            return w[:, :, cols], WLO[:, SLOT_OF["in", c] % NSLOT, :, cols], 2 * SPLIT.index(name) + half

        def gate_unit(n):
            _, c, j = UNITS[n]
            w = slot(("in", c)).rearrange("p (k n) -> p k n", k=KD)
            cols = slice(j * P, (j + 1) * P)
            return w[:, :, cols], WLO[:, SLOT_OF["in", c] % NSLOT, :, cols], SPLIT_G.index(n)

        def round_count(eng):
            eng.wait_ge(row_done, 1)
            return ROW[0:1, RTAB:RTAB + 1]

        @block.sync
        def _(sp):
            sp.dma_start(C[:], cols).then_inc(in_cols, 16)
            wi = w_in.rearrange("(p k) n -> p k n", k=KD)
            wa = w_ada.rearrange("(p k) n -> p k n", k=KD)
            order = {n: i for i, n in enumerate(["q", "k", "v", "u", "gb", "gc", "qc", "zf", "zb", "ic", "oc"])}
            for n, (src, i) in enumerate(STREAM):
                if n == NSLOT:
                    sp.dma_start(X, x.rearrange("(m p) d -> p m d", p=P)).then_inc(in_x, 16)
                if n == NSLOT + 1:
                    sp.dma_start(K[:], consts).then_inc(in_small, 16)
                if n >= NSLOT:
                    free_after(sp, STREAM[n - NSLOT])
                dst = ring[:, n % NSLOT, :]
                if src == "ada":
                    a = wa[:, :, i * WCH:(i + 1) * WCH]
                    sp.dma_start(dst.rearrange("p (k n) -> p k n", k=KD), a).then_inc(loaded[n % NSLOT], 16)
                elif src == "in":
                    i = order.get(IN_CHUNKS[i], i)
                    a = wi[:, :, i * WCH:(i + 1) * WCH]
                    sp.dma_start(dst.rearrange("p (k n) -> p k n", k=KD), a).then_inc(loaded[n % NSLOT], 16)
                elif src == "br":
                    a = w_br[i].rearrange("(k p) n -> p k n", p=P)
                    sp.dma_start(dst.rearrange("p (k n) -> p k n", k=4), a).then_inc(loaded[n % NSLOT], 16)
                elif src == "out":
                    if i == 0:
                        sp.wait_ge(ho_ready, NT)
                        sp.dma_start(WR, w_router.rearrange("(p k) e -> p k e", k=KD)).then_inc(fin_loaded, 16)
                        sp.dma_start(BR, b_router.partition_broadcast(P)).then_inc(fin_loaded, 16)
                        sp.dma_start(FG, final_g.partition_broadcast(P)).then_inc(fin_loaded, 16)
                    a = w_out.rearrange("(k p) n -> p k n", p=P)[:, :, i * WCH:(i + 1) * WCH]
                    sp.dma_start(dst.rearrange("p (k n) -> p k n", k=KD), a).then_inc(loaded[n % NSLOT], 16)
                elif src == "sh":
                    d3 = dst.rearrange("p (k n) -> p k n", k=KD)
                    sp.dma_start(d3[:, :, 0:DE], w_sh_gate.rearrange("(p k) n -> p k n", k=KD)).then_inc(sh_loaded, 16)
                    sp.dma_start(d3[:, :, DE:2 * DE], w_sh_up.rearrange("(p k) n -> p k n", k=KD)).then_inc(sh_loaded, 16)
                else:
                    sp.dma_start(dst[:, 0:2 * D].rearrange("p (k n) -> p k n", k=2),
                                 w_sh_down.rearrange("(k p) n -> p k n", p=P)).then_inc(sh_loaded, 16)

            wg = w_gate.rearrange("e (p k) n -> e p k n", k=KD)
            wu = w_up.rearrange("e (p k) n -> e p k n", k=KD)
            wd = w_down.rearrange("e (k p) n -> e p k n", p=P)

            def experts(r, q):
                e = sp.value_load(ROW[0:1, bass.ds(r, 1)], min_val=0, max_val=NE - 1)
                one = lambda a: a[bass.ds(e, 1)].rearrange("o p k n -> p (o k) n")
                sp.dma_start(GU_W[q][:, :, 0:DE], one(wg)).then_inc(gu_loaded[q], 16)
                sp.dma_start(GU_W[q][:, :, DE:2 * DE], one(wu)).then_inc(gu_loaded[q], 16)
                sp.dma_start(DN_W[q], one(wd)).then_inc(dn_loaded[q], 16)

            sp.wait_ge(row_done, 1)
            rounds = sp.value_load(round_count(sp), min_val=1, max_val=ROUNDS)
            sp.wait_ge(n2_out, 64)
            experts(0, 0)
            sp.wait_ge(shd_ready, NT)
            experts(1, 1)
            experts(2, 2)
            with sp.Fori(0, PASSES) as pas:
                with sp.If(pas * BODY + 1 <= rounds):
                    for p in range(BODY):
                        i = pas * BODY + (1 + p)
                        with sp.If(i + 2 <= rounds):
                            sp.wait_ge(dn_ready, i)
                            experts(i + 2, p % WS)
            sp.wait_ge(scat, rounds * 16 + 16)
            for m in range(NT):
                sp.dma_start(YF[:, m, :], y_rows[m * P:(m + 1) * P, :]).then_inc(y_back[m], 16)
            for m in range(NT):
                sp.wait_ge(fin_done, m + 1)
                sp.dma_start(y[m * P:(m + 1) * P, :], YN[:, m, :]).then_inc(out_done, 16)
            sp.wait_ge(out_done, 16 * NT)
            sp.wait_ge(cache_out, 32)
            sp.wait_ge(state_out, 32)

        @block.scalar
        def _(act):
            chain = [0]

            def link(ins):
                chain[0] += 1
                ins.then_inc(act_order, 1)
                act.wait_ge(act_order, chain[0])

            act.dma_start(CK, cache_k).then_inc(in_cache, 16)
            act.dma_start(CV, cache_v).then_inc(in_cache, 16)
            for ev in SCHEDULE:
                st = ev[0]
                if st == "csilu":
                    act.wait_ge(in_cols, 16)
                    nc.scalar.activation(csil[:, :, :].rearrange("p k v -> p v k"),
                                         cc(C_C).rearrange("p (v k) -> p v k", v=2), ACT.Silu).then_inc(csil_ready, 1)
                elif st == "norm1":
                    act.wait_ge(in_x, 16)
                    for m in range(NT):
                        nc.scalar.activation(XN[:, m, :], X[:, m, :], ACT.Square,
                                             accum_out=small[:, m:m + 1]).then_inc(ssq_done, 1)
                    act.wait_ge(ssq_of, 1)
                    nc.scalar.activation(small[:, 8:8 + NT], small[:, 4:4 + NT], ACT.Sqrt).then_inc(root_done, 1)
                elif st == "unit":
                    n = ev[1]
                    name, c, j = UNITS[n]
                    ps = PS[:, n % 2, :]
                    act.wait_ge(unit_ready, n + 1)
                    if name == "g0":
                        act.wait_ge(cache_out, 32)
                        act.wait_ge(nmove_done, 1)
                    if name == "ada":
                        if c < 4:
                            out = ADA[0:2, c * WCH:(c + 1) * WCH]
                        elif c < 6:
                            if c == 4:
                                act.wait_ge(st_done, 3)
                            out = GR[0:2, (c - 4) * WCH:(c - 3) * WCH]
                        elif c < 10:
                            out = Zrows[:, (c - 6) * WCH:(c - 5) * WCH]
                        else:
                            out = GR[0:2, (c - 8) * WCH:(c - 7) * WCH]
                        nc.scalar.activation(out, ps[0:2, :], ACT.Copy).then_inc(unit_taken, 1)
                        continue
                    if name == "v":
                        act_out, src = V[:, j, :], ps
                    elif name == "ic":
                        act_out, src = IC[:, j, :], ps
                    elif name == "q":
                        nc.scalar.activation(Q[:, j, 0:CTX], ps[:, 0:CTX], ACT.Copy, scale=DH ** -0.5)
                        act_out = Q[:, j, CTX:T].rearrange("p (r c) -> p r c", c=GRID_W)[:, :, ::-1]
                        src = ps[:, CTX:T].rearrange("p (r c) -> p r c", c=GRID_W)
                        nc.scalar.activation(act_out, src, ACT.Copy, scale=DH ** -0.5).then_inc(unit_taken, 1)
                        continue
                    else:
                        src = ps[:, 0:T]
                        if name == "k":
                            act_out = KT[:, j, :]
                        elif name == "u":
                            act_out = UU[:, j, :]
                        elif name == "gb":
                            act_out = GB[:, j, :]
                        elif name == "gc":
                            act_out = GC[:, j, 0:T]
                        elif name == "qc":
                            act_out = QC[:, j, :]
                        elif name == "zf":
                            act_out = Z[:, 0, j, :]
                        elif name == "zb":
                            act_out = Z[:, 1, j, :]
                        elif name == "oc":
                            act_out = OG[:, j, :]
                        else:
                            act_out = G[:, (c - 11) * 4 + j, :]
                    nc.scalar.activation(act_out, src, ACT.Copy).then_inc(unit_taken, 1)
                elif st == "n_high":
                    act.wait_ge(n_ready, KD)
                    nc.scalar.activation(NHI, nT[:, :, :], ACT.Copy).then_inc(nhi_done, 1)
                elif st == "n_move":
                    nc.scalar.activation(NHI2, NHI.bitcast(F32), ACT.Copy).then_inc(nmove_done, 1)
                elif st == "split_g":
                    n = ev[1]
                    w, low, i = gate_unit(n)
                    arrived(act, ("in", UNITS[n][1]))
                    if i < 2:
                        act.wait_ge(cache_out, 32)
                    else:
                        act.wait_ge(unit_ready, n - 1)
                    nc.scalar.activation(GHI[i % 2], w, ACT.Copy).then_inc(ghi_done, 1)
                elif st == "split":
                    w, low, i = half_of(*ev[1:])
                    arrived(act, ("in", IN_CHUNKS.index(ev[1])))
                    if i < 2:
                        act.wait_ge(n_ready, KD)
                    else:
                        act.wait_ge(unit_ready, AFTER[SPLIT[i // 2 - 1]] - (2 if i % 2 == 0 else 0))
                    nc.scalar.activation(WHI[:, i % 2, :, :], w, ACT.Copy).then_inc(whi_done, 1)
                elif st == "cache":
                    act.wait_ge(ck_t, 1)
                    nc.scalar.activation(CKT.rearrange("p j t -> p (j t)"), PS[:, 4, :], ACT.Copy).then_inc(ck_taken, 1)
                    act.wait_ge(ck_t, 2)
                    nc.scalar.activation(CKO, PS[:, 5, :], ACT.Copy).then_inc(ck_taken, 1)
                    act.wait_ge(ck_taken, 2)
                    act.dma_start(new_k, CKO).then_inc(cache_out, 16)
                    act.wait_ge(unit_taken, AFTER["v"])
                    act.dma_start(new_v, V[:, 0, :]).then_inc(cache_out, 16)
                elif st == "scores":
                    h = ev[1]
                    for u in range(3):
                        i = 3 * h + u
                        act.wait_ge(max_ready, i + 1)
                        w = P if u == 2 else T
                        if h > 0 and u == 0:
                            act.wait_ge(pt_ready, 3 * h)
                        nc.scalar.activation(PR[:, u, 0:w], SB[:, u, 0:w], ACT.Exp, bias=small[:, 16 + u:17 + u],
                                             accum_out=small[:, 20 + u:21 + u]).then_inc(exp_ready, 1)
                elif st == "values":
                    h = ev[1]
                    for u in range(3):
                        i = 3 * h + u
                        act.wait_ge(pt_ready, i + 1)
                        if u == 0 and h > 0:
                            act.wait_ge(pv_ready, h)
                        if u < 2:
                            nc.scalar.activation(PT[:, :, u * P:(u + 1) * P],
                                                 PS[:, 4, 0:T].rearrange("p (k t) -> p k t", k=3), ACT.Copy).then_inc(pt_taken, 1)
                        else:
                            nc.scalar.activation(PTC, PS[:, 4, 0:P], ACT.Copy).then_inc(pt_taken, 1)
                    o = 64 * (h % 2)
                    act.wait_ge(pv_ready, h + 1)
                    nc.scalar.activation(OA[o:o + DH, h // 2, CTX:T].rearrange("p (r c) -> p r c", c=GRID_W)[:, :, ::-1],
                                         PS[o:o + DH, 5, 0:2 * P].rearrange("p (r c) -> p r c", c=GRID_W),
                                         ACT.Copy)
                    nc.scalar.activation(OA[o:o + DH, h // 2, 0:CTX], PS[o:o + DH, 5, 2 * P:3 * P], ACT.Copy).then_inc(pv_taken, 1)
                elif st == "gates":
                    act.wait_ge(conv_done, 4)
                    act.wait_ge(pv_ready, NH)
                    for d in range(2):
                        act.dma_start(ST[:, d, :, :], state[d].rearrange("h k v -> k h v")).then_inc(in_state, 16)
                    act.wait_ge(unit_taken, AFTER["zb"])
                    link(nc.scalar.activation(KEY, Z, ACT.Sigmoid, scale=-1.0))
                    nc.scalar.activation(Z, Z, ACT.Sigmoid).then_inc(sig_done, 1)
                elif st == "decays":
                    act.wait_ge(f_done, 1)
                    nc.scalar.activation(Z, Z, ACT.Ln).then_inc(logf_done, 1)
                elif st == "ops":
                    if ev[1] % 8 < 7:
                        act.wait_ge(diff_done, ev[1] - ev[1] // 8 + 1)
                        nc.scalar.activation(E, E, ACT.Exp).then_inc(edec_done, 1)
                elif st == "carry":
                    act.wait_ge(diff_done, 15)
                    act.wait_ge(b_done, 1)
                    act.wait_ge(nback_done, KD)
                    link(nc.scalar.activation(KH, KH, ACT.Exp))
                    nc.scalar.activation(EB, Z[:, :, :, CTX:T], ACT.Exp).then_inc(edec_done, 1)
                elif st == "carry_t":
                    for c in range(4):
                        act.wait_ge(kht_ready, c + 1)
                        nc.scalar.activation(KHT[:, c, :, :].rearrange("p h t -> p (h t)"), PS[:, 4 + c % 2, :],
                                             ACT.Copy).then_inc(kht_taken, 1)
                elif st == "hout":
                    m = ev[1]
                    act.wait_ge(ho_ready, m + 1)
                    if m > 0:
                        act.wait_ge(ho_norm, m)
                    nc.scalar.activation(OS, PS[:, 6, :], ACT.Copy).then_inc(ho_taken, 1)
                    act.wait_ge(ho_ms, m + 1)
                    nc.scalar.activation(small[:, 36:40], small[:, 32:36], ACT.Sqrt).then_inc(ho_root, 1)
                    if m == 0:
                        act.wait_ge(unit_taken, AFTER["oc"])
                        nc.scalar.activation(OG, OG, ACT.Silu).then_inc(late_done, 1)
                        for d in range(2):
                            act.dma_start(new_state[d].rearrange("h k v -> k h v"), STC[:, d, :, :]).then_inc(state_out, 16)
                elif st == "late_act":
                    b = ev[1]
                    if b == 0:
                        act.wait_ge(unit_taken, AFTER["g5"])
                        act.wait_ge(ho_ready, NT)
                        act.dma_start(XH, x.rearrange("(m p) d -> p m d", p=P)).then_inc(in_xh, 16)
                        act.dma_start(BG[0:2, :], b_gate).then_inc(bg_loaded, 16)
                    g = G[:, 8 * b:8 * b + 8, :]
                    nc.scalar.activation(g, g, ACT.Sigmoid).then_inc(late_done, 1)
                elif st == "gate2":
                    act.wait_ge(hot_ready, NT)
                    act.wait_ge(state_out, 32)
                    for i in range(4):
                        v, hf = i // 2, i % 2
                        act.wait_ge(g2_ready, i + 1)
                        nc.scalar.activation(GBC[:, 1, v, hf * 512:(hf + 1) * 512], PS[:, 2 + i, :], ACT.Copy).then_inc(g2_taken, 1)
                elif st == "norm2":
                    m = ev[1]
                    act.wait_ge(wo_taken, 2 * m + 2)
                    nc.scalar.activation(XN2[:, m, :], XH[:, m, :], ACT.Square,
                                         accum_out=small[:, m:m + 1]).then_inc(ssq2, 1)
                    act.wait_ge(ms2, m + 1)
                    nc.scalar.activation(small[:, 8 + m:9 + m], small[:, 4 + m:5 + m], ACT.Sqrt).then_inc(root2, 1)
                elif st == "rows":
                    m = ev[1]
                    for hf in range(2):
                        act.wait_ge(n2t_ready, 2 * m + hf + 1)
                        dst = N2[:, m, :].rearrange("p (f k) -> p k f", k=KD)[:, 4 * hf:4 * hf + 4, :]
                        nc.scalar.activation(dst, PS[:, 2 + hf, :].rearrange("p (k f) -> p k f", k=4), ACT.Copy).then_inc(n2_rowed, 1)
                    act.wait_ge(n2_rowed, 2 * m + 2)
                    act.dma_start(n2_rows[m * P:(m + 1) * P, :], N2[:, m, :]).then_inc(n2_out, 16)
                    if m == 0:
                        act.dma_start(n2_rows[T:T + P, :], N2[:, 0, :]).then_inc(n2_out, 16)
                elif st == "router":
                    act.wait_ge(rt_ready, 1)
                    nc.scalar.activation(SG, PS[:, 6, 0:NT * NE].rearrange("p (m e) -> p m e", m=NT), ACT.Sigmoid).then_inc(rt_sig, 1)
                elif st == "table_t":
                    act.wait_ge(te_ready, 1)
                    nc.scalar.activation(TE[0:NE, 0:4, :], PS[0:NE, 6, :].rearrange("p (a t) -> p a t", a=4), ACT.Copy)
                    nc.scalar.activation(TE[0:NE, 4:7, :], PS[0:NE, 7, 0:T].rearrange("p (a t) -> p a t", a=3), ACT.Copy).then_inc(te_taken, 1)
                elif st == "table":
                    act.wait_ge(pr_ready, 1)
                    nc.scalar.activation(COMB, PS[:, 6, 0:T].rearrange("p (m r) -> p m r", m=NT), ACT.Copy).then_inc(comb_done, 1)
                elif st == "sh_up":
                    m = ev[1]
                    act.wait_ge(sg_ready, m + 1)
                    if m >= 2:
                        act.wait_ge(sh_hid, m - 1)
                    nc.scalar.activation(HS[:, m % 2, :], PS[:, 4 + min(m, 1), 0:DE], ACT.Silu).then_inc(ss_done, 1)
                elif st == "sh_down":
                    m = ev[1]
                    act.wait_ge(sht_ready, m + 1)
                    nc.scalar.activation(HT[:, m % 2, :, :], PS[:, 0, 0:2 * P].rearrange("p (k t) -> p k t", k=2), ACT.Copy).then_inc(sht_taken, 1)
                    act.wait_ge(shd_ready, m + 1)
                    nc.scalar.activation(SHO[:, m, :].rearrange("p (a n) -> p a n", a=2), PS[:, 1:3, :], ACT.Copy).then_inc(sho_done, 1)
                    act.wait_ge(sho_done, m + 1)
                    act.dma_start(y_rows[m * P:(m + 1) * P, :], SHO[:, m, :]).then_inc(y_init, 16)

            def take_xt(r, b):
                act.wait_ge(xg_t, r + 1)
                nc.scalar.activation(XT[:, b, :, :].rearrange("p (a k) t -> p a (k t)", a=2), PS[:, 0:2, :], ACT.Copy).then_inc(xt_done, 1)

            def silu(r, b):
                act.wait_ge(gu_ready, r + 1)
                nc.scalar.activation(HS[:, b, :], PS[:, 2 + b, 0:DE], ACT.Silu).then_inc(silu_done, 1)

            rounds = act.value_load(round_count(act), min_val=1, max_val=ROUNDS)
            take_xt(0, 0)
            take_xt(1, 1)
            silu(0, 0)
            with act.Fori(0, PASSES) as pas:
                with act.If(pas * BODY + 1 <= rounds):
                    for p in range(BODY):
                        i = pas * BODY + (1 + p)
                        with act.If(i <= rounds):
                            act.wait_ge(gu_ready, i)
                            take_xt(i + 1, p % 2)
                            act.wait_ge(ht_ready, i)
                            nc.scalar.activation(HT[:, p % 2, :, :], PS[:, 5, 0:2 * P].rearrange("p (k t) -> p k t", k=2),
                                                 ACT.Copy).then_inc(ht_done, 1)
                            act.wait_ge(hid_done, i)
                            silu(i, (1 + p) % 2)
            for m in range(NT):
                act.wait_ge(h2_done, m + 1)
                nc.scalar.activation(YN[:, m, :], YF[:, m, :], ACT.Square, accum_out=small[:, m:m + 1]).then_inc(ssq3, 1)
                act.wait_ge(ms3, m + 1)
                nc.scalar.activation(small[:, 8 + m:9 + m], small[:, 4 + m:5 + m], ACT.Sqrt).then_inc(root3, 1)

        @block.gpsimd
        def _(pool):
            chain = [0]

            def link(ins):
                chain[0] += 1
                ins.then_inc(pool_order, 1)
                pool.wait_ge(pool_order, chain[0])

            link(nc.gpsimd.memset(BIAS, 0.0))
            pool.wait_ge(in_small, 16)
            for h in range(NH):
                b = h % 2
                if h >= 2:
                    pool.wait_ge(s_taken, 3 * (h - 1))
                for qr in range(4):
                    src = bass.AP(rpb.tensor, h * 15 * 31 + (7 - qr) * 31 - 48, [[1, GRID_W], [31, 4], [1, GRID_W]])
                    o = 64 * (qr % 2)
                    pool.dma_start(BIAS[o:o + 64, b, qr // 2, 0:256].rearrange("p (r c) -> p r c", r=4), src)\
                        .then_inc(in_bias[b], 16)
                pool.wait_ge(in_bias[b], 64 * (h // 2 + 1))
                for t in range(2):
                    v = BIAS[:, b, t, 0:256].rearrange("p (r c) -> p r c", r=4)
                    nc.gpsimd.tensor_tensor(v, v, kc(K_MASK).unsqueeze(1).broadcast_to([P, 4, GRID_W]), ALU.add)\
                        .then_inc(bias_masked, 1)

            pool.wait_ge(conv_done, 4)
            nc.gpsimd.memset(AT_, 0.0).then_inc(at_zero, 1)

            for n in SPLIT_G:
                w, low, i = gate_unit(n)
                pool.wait_ge(ghi_done, i + 1)
                nc.gpsimd.tensor_tensor(low, w, GHI[i % 2].bitcast(F32), ALU.subtract).then_inc(glo_done, 1)

            def gather(r, p):
                pool.wait_ge(idx_done, r + 1)
                pool.sem_inc(gather_go, 1)
                pool.indirect_dma_start(XG[:, p % XGS, :], None, n2_rows,
                                        bass.IndirectOffsetOnAxis(ap=IDX[:, p:p + 1], axis=0)).then_inc(gathered[p % XGS], 16)

            pool.wait_ge(n2_out, 64)
            for r in range(XGS):
                gather(r, r)
            pool.wait_ge(xg_t, 1)
            gather(XGS, XGS)
            pool.wait_ge(sho_done, 1)
            pool.dma_start(y_rows[T:T + P, :], SHO[:, 0, :]).then_inc(scat, 16)
            pool.wait_ge(y_init, 16 * NT)
            pool.sem_inc(added, 1)
            rounds = pool.value_load(round_count(pool), min_val=1, max_val=ROUNDS)
            with pool.Fori(0, PASSES) as pas:
                with pool.If(pas * BODY + 1 <= rounds):
                    for p in range(BODY):
                        i = pas * BODY + (1 + p)
                        with pool.If(i <= rounds):
                            pool.wait_ge(xg_t, i + 1)
                            gather(i + AHEAD, (1 + p + AHEAD) % BODY)
                            pool.wait_ge(ys_done, i + 1)
                            pool.wait_ge(scat, 16 * i)
                            pool.sem_inc(added, 1)
                            pool.indirect_dma_start(y_rows, bass.IndirectOffsetOnAxis(ap=IDX[:, p:p + 1], axis=0),
                                                    YS[:, p % 2, :], None, compute_op=ALU.add).then_inc(scat, 16)

        @block.vector
        def _(dve):
            chain = [0]

            def link(ins):
                chain[0] += 1
                ins.then_inc(dve_order, 1)
                dve.wait_ge(dve_order, chain[0])

            def rsqrt_fix(ms, root, r, t):
                link(nc.vector.reciprocal(r, root))
                link(nc.vector.tensor_tensor(t, r, r, ALU.mult))
                link(nc.vector.tensor_tensor(t, t, ms, ALU.mult))
                link(nc.vector.tensor_scalar(t, t, -0.5, 1.5, ALU.mult, ALU.add))
                link(nc.vector.tensor_tensor(r, r, t, ALU.mult))

            def one_hots(r, b):
                for m in range(NT):
                    nc.vector.tensor_scalar(OH[:, b, m, :], kc(K_R128), POSR[:, m, bass.ds(r, 1)], None, ALU.is_equal)
                nc.vector.tensor_copy(RHS[:, b, :, 2:3], COMB[:, :, bass.ds(r, 1)])
                nc.vector.tensor_copy(RHS[:, b, :, 3:4], COMBL[:, :, bass.ds(r, 1)]).then_inc(oh_done, 1)

            def take_index(r, p):
                dve.wait_ge(ix_ready, r + 1)
                ix = PS[:, 4, 0:4]
                link2(nc.vector.tensor_scalar(NCNT, ix[:, 1:2], -1.0, 1.0, ALU.mult, ALU.add), r + 1)
                nc.vector.tensor_reduce(WC[:, p:p + 1], ix[:, 2:4], AX.X, ALU.add)
                nc.vector.scalar_tensor_tensor(IDX[:, p:p + 1], NCNT, kc(K_COL)[:, 1:2], ix[:, 0:1],
                                               ALU.mult, ALU.add).then_inc(idx_done, 1)

            def link2(ins, n):
                ins.then_inc(prep_order, 1)
                dve.wait_ge(prep_order, n)

            def modulate(which, ready, done):
                for k in range(KD):
                    dve.wait_ge(ready, k + 1)
                    nc.vector.tensor_scalar(nT[:, k, 0:CTX], PS[:, 2 + k % 4, 0:CTX], modc[:, which + 1, 0, k:k + 1],
                                            modc[:, which, 0, k:k + 1], ALU.mult, ALU.add).then_inc(dve_order, 1)
                    chain[0] += 1
                    nc.vector.tensor_scalar(nT[:, k, CTX:T], PS[:, 2 + k % 4, CTX:T], modc[:, which + 1, 1, k:k + 1],
                                            modc[:, which, 1, k:k + 1], ALU.mult, ALU.add).then_inc(done, 1)
                dve.wait_ge(done, KD)
                dve.wait_ge(dve_order, chain[0])

            def mod_columns(which, bank, nvec, norm, cnt):
                src = PS[:, bank, 0:32].rearrange("p (s k v) -> p s v k", s=2, v=2)
                b = cc(C_ADA).rearrange("p (s k) -> p s k", s=4)
                for s in range(2):
                    link(nc.vector.tensor_tensor(modc[:, which + s, :, :], src[:, s, :, :],
                                                 b[:, which + s, :].unsqueeze(1).broadcast_to([P, 2, KD]), ALU.add))
                link(nc.vector.tensor_scalar(modc[:, which + 1, :, :], modc[:, which + 1, :, :], 1.0, None, ALU.add))
                nc.vector.tensor_tensor(modc[:, which + 1, :, :], modc[:, which + 1, :, :],
                                        norm.unsqueeze(1).broadcast_to([P, 2, KD]), ALU.mult).then_inc(mod_ready, 1)
                dve.wait_ge(mod_ready, cnt)

            def take_level(i):
                dve.wait_ge(lev_ready, i + 1)
                if i == 0:
                    dve.wait_ge(at_zero, 1)
                if i > 0:
                    dve.wait_ge(lev_taken, i)
                mask = levmask[:, i % 8, :] if i % 8 < 7 else ident.bitcast(U32)
                for hh in range(2):
                    ins = nc.vector.copy_predicated(AT_[:, 2 * (i // 8) + hh, :, :], mask.unsqueeze(1).broadcast_to([P, NT, P]),
                                                    PS[:, 6 + hh, 0:T].rearrange("p (m t) -> p m t", m=NT))
                ins.then_inc(lev_taken, 1)

            dve.sem_inc(hid_done, 1)
            dve.sem_inc(ys_done, 1)
            for ev in SCHEDULE:
                st = ev[0]
                if st == "norm1":
                    dve.wait_ge(ssq_done, NT)
                    nc.vector.tensor_scalar(small[:, 4:4 + NT], small[:, 0:NT], 1.0 / D, EPS, ALU.mult, ALU.add).then_inc(ssq_of, 1)
                    dve.wait_ge(ssq_of, 1)
                    dve.wait_ge(root_done, 1)
                    rsqrt_fix(small[:, 4:4 + NT], small[:, 8:8 + NT], small[:, 12:12 + NT], small[:, 24:24 + NT])
                    for m in range(NT):
                        nc.vector.tensor_scalar(XN[:, m, :], X[:, m, :], small[:, 12 + m:13 + m], None, ALU.mult).then_inc(xn_ready, 1)
                elif st == "n_low":
                    dve.wait_ge(nhi_done, 1)
                    dve.wait_ge(unit_ready, AFTER["ic"])
                    for k in range(KD):
                        nc.vector.tensor_tensor(NLO[:, k, :], nT[:, k, :], NHI[:, k, :].bitcast(F32), ALU.subtract).then_inc(nlo_done, 1)
                elif st == "n_back":
                    dve.wait_ge(nlo_done, KD)
                    dve.wait_ge(nmove_done, 1)
                    dve.wait_ge(unit_ready, SPLIT_G[-1] + 1)
                    for k in range(KD):
                        nc.vector.tensor_tensor(nT[:, k, :], NLO[:, k, :].bitcast(F32), NHI2[:, k, :].bitcast(F32), ALU.add).then_inc(nback_done, 1)
                elif st == "split":
                    w, low, i = half_of(*ev[1:])
                    dve.wait_ge(whi_done, i + 1)
                    nc.vector.tensor_tensor(low, w, WHI[:, i % 2, :, :].bitcast(F32), ALU.subtract).then_inc(wlo_done, 1)
                elif st == "mod1":
                    dve.wait_ge(in_cols, 16)
                    dve.wait_ge(modt_ready, 1)
                    mod_columns(0, 7, 2, cc(C_N1), 1)
                    modulate(0, xnt_ready, n_ready)
                elif st == "scores":
                    h = ev[1]
                    for u in range(3):
                        i = 3 * h + u
                        dve.wait_ge(s_ready, i + 1)
                        if h > 0:
                            dve.wait_ge(exp_ready, 3 * h)
                        if u < 2:
                            dve.wait_ge(bias_masked, 2 * h + 2)
                            nc.vector.tensor_tensor(SB[:, u, :], PS[:, 2 + i % 2, 0:T], BIAS[:, h % 2, u, :], ALU.add).then_inc(s_taken, 1)
                            w = T
                        else:
                            nc.vector.tensor_copy(SB[:, 2, 0:P], PS[:, 2 + i % 2, 0:P]).then_inc(s_taken, 1)
                            w = P
                        dve.wait_ge(s_taken, i + 1)
                        nc.vector.tensor_reduce(small[:, 16 + u:17 + u], SB[:, u, 0:w], AX.X, ALU.max,
                                                negate=True).then_inc(max_ready, 1)
                    for u in range(3):
                        i = 3 * h + u
                        w = P if u == 2 else T
                        dve.wait_ge(exp_ready, i + 1)
                        link(nc.vector.reciprocal(small[:, 28 + u:29 + u], small[:, 20 + u:21 + u]))
                        nc.vector.tensor_scalar(PR[:, u, 0:w], PR[:, u, 0:w], small[:, 28 + u:29 + u], None,
                                                ALU.mult).then_inc(prob_ready, 1)
                    dve.wait_ge(prob_ready, 3 * h + 3)
                elif st == "conv":
                    j = ev[1]
                    if j == 0:
                        dve.wait_ge(unit_taken, AFTER["gc"])
                        nc.vector.memset(ZP[:, :, 0:1], 0.0)
                        nc.vector.memset(ZP[:, :, 1 + CTX:3 + CTX], 0.0)
                        link(nc.vector.memset(ZP[:, :, 3 + T:4 + T], 0.0))
                    wv = cc(C_CONV).rearrange("p (w j) -> p w j", w=3)
                    nc.vector.tensor_tensor(ZP[:, j, 1:1 + CTX], GC[:, j, 0:CTX], UU[:, j, 0:CTX], ALU.mult)
                    link(nc.vector.tensor_tensor(ZP[:, j, 3 + CTX:3 + T], GC[:, j, CTX:T], UU[:, j, CTX:T], ALU.mult))
                    acc = GC[:, j, 1:387]
                    link(nc.vector.tensor_scalar(acc, ZP[:, j, 1:387], wv[:, 1, j:j + 1], None, ALU.mult))
                    link(nc.vector.scalar_tensor_tensor(acc, ZP[:, j, 0:386], wv[:, 0, j:j + 1], acc, ALU.mult, ALU.add))
                    link(nc.vector.scalar_tensor_tensor(acc, ZP[:, j, 2:388], wv[:, 2, j:j + 1], acc, ALU.mult, ALU.add))
                    nc.vector.tensor_tensor(GB[:, j, 0:CTX], GB[:, j, 0:CTX], GC[:, j, 1:1 + CTX], ALU.mult)
                    nc.vector.tensor_tensor(GB[:, j, CTX:T], GB[:, j, CTX:T], GC[:, j, 3 + CTX:3 + T], ALU.mult).then_inc(conv_done, 1)
                    dve.wait_ge(conv_done, j + 1)
                elif st == "gates":
                    lbr, lb = cc(C_LB), small[:, 48:56]
                    omlb, lbf, e8 = small[:, 56:64], small[:, 64:72], small[:, 72:80]
                    link(nc.vector.tensor_tensor(lb, lbr, lbr, ALU.subtract))
                    link(nc.vector.tensor_scalar(lb, lb, 1.0, None, ALU.add))
                    link(nc.vector.reciprocal(e8, lb))
                    link(nc.vector.tensor_tensor(e8, lb, e8, ALU.mult))
                    link(nc.vector.tensor_tensor(lb, e8, e8, ALU.subtract))
                    link(nc.vector.tensor_scalar(omlb, lb, -1.0, 1.0, ALU.mult, ALU.add))
                    link(nc.vector.tensor_scalar(lbf, lb, LOG_FLOOR, None, ALU.max))
                    dve.wait_ge(sig_done, 1)
                    for d in range(2):
                        for h in range(HC):
                            q = 4 * d + h
                            nc.vector.tensor_scalar(KEY[:, d, h, :], KEY[:, d, h, :], omlb[:, q:q + 1], None, ALU.mult).then_inc(dve_order, 1)
                            nc.vector.tensor_scalar(Z[:, d, h, :], Z[:, d, h, :], omlb[:, q:q + 1], lbf[:, q:q + 1],
                                                    ALU.mult, ALU.add).then_inc(dve_order, 1)
                            chain[0] += 2
                    dve.wait_ge(dve_order, chain[0])
                    link(nc.vector.tensor_copy(small[:, 80:81], small[:, 56:57]))
                    nc.vector.tensor_copy(small[:, 81:82], small[:, 56:57]).then_inc(f_done, 1)
                elif st == "sums":
                    dve.wait_ge(logf_done, 1)
                    scan = kc(K_SCAN)
                    for h in range(HC):
                        nc.vector.tensor_tensor_scan(Z[:, 0, h, :], scan, Z[:, 0, h, :], 0.0, ALU.mult, ALU.add).then_inc(dve_order, 1)
                        nc.vector.tensor_tensor_scan(Z[:, 1, h, ::-1], scan, Z[:, 1, h, ::-1], 0.0, ALU.mult, ALU.add).then_inc(dve_order, 1)
                        chain[0] += 2
                    dve.wait_ge(dve_order, chain[0])
                    nc.vector.tensor_copy(small[:, 82:83], small[:, 56:57]).then_inc(b_done, 1)
                elif st == "ops":
                    i = ev[1]
                    h2, l = i // 8, i % 8
                    hs = slice(2 * h2, 2 * h2 + 2)
                    if i == 0:
                        dve.wait_ge(pv_ready, NH)
                        dve.wait_ge(cache_out, 32)
                    else:
                        dve.wait_ge(qk_done, i)
                    if l < 7:
                        L = LEVELS[l]
                        nb, hf = 2 * T // L, L // 2
                        cutb = lambda a: a.rearrange("p (n l) -> p n l", l=L)
                        zz = [Z[:, d, hs, :].rearrange("p h t -> p (h t)") for d in range(2)]
                        ref = [cutb(zz[0])[:, :, hf - 1:hf], cutb(zz[1])[:, :, hf:hf + 1]]
                        for d, right in ((0, True), (0, False), (1, True), (1, False)):
                            s = slice(hf, L) if right else slice(0, hf)
                            tok, mid = cutb(zz[d])[:, :, s], ref[d].broadcast_to([P, nb, hf])
                            a, c = (tok, mid) if right == (d == 0) else (mid, tok)
                            ins = nc.vector.tensor_tensor(cutb(E[:, d, :])[:, :, s], a, c, ALU.subtract)
                        ins.then_inc(diff_done, 1)
                    if i > 0:
                        take_level(i - 1)
                    if l < 7:
                        dve.wait_ge(edec_done, 7 * h2 + l + 1)
                        qq = QC[:, hs, :].rearrange("p h t -> p (h t)")
                        kk = [KEY[:, d, hs, :].rearrange("p h t -> p (h t)") for d in range(2)]
                        for out, a, d, right in ((QX, qq, 0, True), (QX, qq, 1, False), (KX, kk[1], 1, True), (KX, kk[0], 0, False)):
                            s = slice(hf, L) if right else slice(0, hf)
                            ins = nc.vector.tensor_tensor(cutb(out)[:, :, s], cutb(a)[:, :, s],
                                                          cutb(E[:, d, :])[:, :, s], ALU.mult)
                    else:
                        nc.vector.tensor_copy(QX, QC[:, hs, :].rearrange("p h t -> p (h t)"))
                        ins = nc.vector.tensor_tensor(KX, KEY[:, 0, hs, :].rearrange("p h t -> p (h t)"),
                                                      KEY[:, 1, hs, :].rearrange("p h t -> p (h t)"), ALU.add)
                    ins.then_inc(qk_done, 1)
                elif st == "carry":
                    take_level(15)
                    for c, (d, m) in enumerate(((0, 0), (1, 0), (0, 1), (1, 2))):
                        last = m * P + (P - 1 if d == 0 else 0)
                        ins = nc.vector.tensor_tensor(KH[:, c, :, :], Z[:, d, :, last:last + 1].broadcast_to([P, HC, P]),
                                                      Z[:, d, :, m * P:(m + 1) * P], ALU.subtract)
                        if c < 3:
                            link(ins)
                        else:
                            ins.then_inc(diff_done, 1)
                    dve.wait_ge(edec_done, 15)
                    for c, (d, m) in enumerate(((0, 0), (1, 0), (0, 1), (1, 2))):
                        nc.vector.tensor_tensor(KH[:, c, :, :], KH[:, c, :, :], KEY[:, d, :, m * P:(m + 1) * P],
                                                ALU.mult).then_inc(kh_done, 1)
                elif st == "carry_products":
                    dve.wait_ge(in_state, 32)
                    for c in range(4):
                        dve.wait_ge(kv_ready, c + 1)
                        kv = PS[:, 6 + c % 2, :].rearrange("p (h v) -> p h v", h=HC)
                        if c < 2:
                            nc.vector.tensor_copy(STC[:, c, :, :], kv).then_inc(st_done, 1)
                            dve.wait_ge(st_done, c + 1)
                        else:
                            d, last = c - 2, (P - 1 if c == 2 else P)
                            for h in range(HC):
                                link(nc.vector.scalar_tensor_tensor(ST2[:, d, h, :], ST[:, d, h, :], EB[:, d, h, last:last + 1],
                                                                    kv[:, h, :], ALU.mult, ALU.add))
                    for d in range(2):
                        link(nc.vector.tensor_tensor(EB[:, d, :, :], EB[:, d, :, :], QC[:, :, CTX:T], ALU.mult))
                    nc.vector.tensor_copy(small[:, 83:84], small[:, 56:57]).then_inc(st_done, 1)
                elif st == "hout":
                    m = ev[1]
                    dve.wait_ge(ho_taken, m + 1)
                    link(nc.vector.tensor_tensor(OQ, OS, OS, ALU.mult))
                    link(nc.vector.tensor_reduce(small[:, 40:44], OQ.rearrange("p (h v) -> p h v", h=HC), AX.X, ALU.add))
                    nc.vector.tensor_scalar(small[:, 32:36], small[:, 40:44], 1.0 / P, EPS, ALU.mult, ALU.add).then_inc(ho_ms, 1)
                    dve.wait_ge(ho_ms, m + 1)
                    dve.wait_ge(ho_root, m + 1)
                    rsqrt_fix(small[:, 32:36], small[:, 36:40], small[:, 44:48], small[:, 88:92])
                    if m > 0:
                        dve.wait_ge(hot_ready, m)
                    nc.vector.tensor_tensor(OR.rearrange("p (h v) -> p h v", h=HC), OS.rearrange("p (h v) -> p h v", h=HC),
                                            small[:, 44:48].unsqueeze(2).broadcast_to([P, HC, P]), ALU.mult).then_inc(ho_norm, 1)
                elif st == "hout_t":
                    m = ev[1]
                    dve.wait_ge(late_done, 1)
                    dve.wait_ge(hot_ready, m + 1)
                    for h in range(HC):
                        ins = nc.vector.scalar_tensor_tensor(OCT[:, h, m * P:(m + 1) * P], PS[:, 7, h * P:(h + 1) * P],
                                                             cc(C_HG)[:, h:h + 1], OG[:, h, m * P:(m + 1) * P], ALU.mult, ALU.mult)
                        if h < HC - 1:
                            link(ins)
                        else:
                            ins.then_inc(hot_taken, 1)
                elif st == "branches":
                    dve.wait_ge(unit_taken, len(UNITS))
                    dve.wait_ge(bg_loaded, 16)
                    nc.vector.tensor_tensor(GR[0:2, :], GR[0:2, :], BG[0:2, :], ALU.add).then_inc(gr_ready, 1)
                    for i in range(24):
                        br, j = i // KD, i % KD
                        if j == 0:
                            dve.wait_ge(late_done, 2 + br)
                        dve.wait_ge(br_ready, i + 1)
                        g = G[:, 8 * br + j, :]
                        nc.vector.tensor_tensor(g, PS[:, i % 6, 0:T], g, ALU.mult).then_inc(br_taken, 1)
                        if br > 0:
                            dve.wait_ge(br_taken, i + 1)
                            nc.vector.tensor_tensor(G[:, j, :], G[:, j, :], g, ALU.add).then_inc(mix_done, 1)
                            if br == 1 and j == KD - 1:
                                dve.wait_ge(mix_done, KD)
                elif st == "mod2":
                    dve.wait_ge(modt_ready, 2)
                    mod_columns(2, 7, 2, cc(C_N2), 2)
                elif st == "gate1":
                    for i in range(4):
                        v, hf = i // 2, i % 2
                        dve.wait_ge(gb_ready, i + 1)
                        nc.vector.tensor_copy(GBC[:, 0, v, hf * 512:(hf + 1) * 512], PS[:, 2 + i, :]).then_inc(gb_taken, 1)
                    dve.wait_ge(gb_taken, 4)
                elif st == "wout":
                    m = ev[1]
                    hf = ev[2]
                    s = slice(hf * 512, (hf + 1) * 512)
                    dve.wait_ge(in_xh, 16)
                    dve.wait_ge(wo_ready, 2 * m + hf + 1)
                    link(nc.vector.tensor_tensor(T1, PS[:, 6 + hf, :], GBC[:, 0, min(m, 1), s], ALU.mult))
                    nc.vector.tensor_tensor(XH[:, m, s], XH[:, m, s], T1, ALU.add).then_inc(wo_taken, 1)
                    dve.wait_ge(wo_taken, 2 * m + hf + 1)
                elif st == "norm2":
                    m = ev[1]
                    col = lambda i: small[:, i + m:i + m + 1]
                    dve.wait_ge(ssq2, m + 1)
                    nc.vector.tensor_scalar(col(4), col(0), 1.0 / D, EPS, ALU.mult, ALU.add).then_inc(ms2, 1)
                    dve.wait_ge(ms2, m + 1)
                    dve.wait_ge(root2, m + 1)
                    rsqrt_fix(col(4), col(8), col(12), col(24))
                    nc.vector.tensor_scalar(XN2[:, m, :], XH[:, m, :], col(12), None, ALU.mult).then_inc(xn2, 1)
                elif st == "norm_t":
                    m = ev[1]
                    dve.wait_ge(xnt2, m + 1)
                    for k in range(KD):
                        ins = nc.vector.tensor_scalar(nT[:, k, m * P:(m + 1) * P], PS[:, k // 4, k % 4 * P:(k % 4 + 1) * P],
                                                      modc[:, 3, min(m, 1), k:k + 1], modc[:, 2, min(m, 1), k:k + 1],
                                                      ALU.mult, ALU.add)
                    ins.then_inc(n2_ready, 1)
                elif st == "router":
                    dve.wait_ge(fin_loaded, 48)
                    dve.wait_ge(rt_sig, 1)
                    link(nc.vector.tensor_tensor(SE, SG, BR.unsqueeze(1).broadcast_to([P, NT, NE]), ALU.add))
                    for m in range(NT):
                        for g in range(NG):
                            ins = nc.vector.max(M8[:, m, g, :], SE[:, m, g * 8:g * 8 + 8])
                    link(ins)
                    link(nc.vector.tensor_tensor(GS, M8[:, :, :, 0], M8[:, :, :, 1], ALU.add))
                    for m in range(NT):
                        other = GS[:, m, :].unsqueeze(1).broadcast_to([P, NG, NG])
                        own = GS[:, m, :].unsqueeze(2).broadcast_to([P, NG, NG])
                        nc.vector.tensor_tensor(CMP[:, m, :, :], other, own, ALU.is_gt)
                        ins = nc.vector.tensor_tensor(CM2[:, m, :, :], other, own, ALU.is_equal)
                    link(ins)
                    flat = lambda a: a.rearrange("p m a b -> p m (a b)")
                    link(nc.vector.tensor_tensor(flat(CM2), flat(CM2), kc(K_T8).unsqueeze(1).broadcast_to([P, NT, NG * NG]), ALU.mult))
                    link(nc.vector.tensor_tensor(CMP, CMP, CM2, ALU.add))
                    link(nc.vector.tensor_reduce(GK, CMP, AX.X, ALU.add))
                    link(nc.vector.tensor_scalar(GK, GK, float(TOPG), None, ALU.is_lt))
                    g4 = lambda a: a.rearrange("p m (g e) -> p (m g) e", g=NG)
                    gk = GK.rearrange("p m g -> p (m g)").unsqueeze(2).broadcast_to([P, NT * NG, 8])
                    link(nc.vector.tensor_tensor(g4(SM), g4(SE), gk, ALU.mult))
                    link(nc.vector.tensor_scalar(GK, GK, -NEG_BIG, NEG_BIG, ALU.mult, ALU.add))
                    link(nc.vector.tensor_tensor(g4(SM), g4(SM), gk, ALU.add))
                    for m in range(NT):
                        ins = nc.vector.max(T8[:, m, :], SM[:, m, :])
                    link(ins)
                    for m in range(NT):
                        ins = nc.vector.match_replace(MK[:, m, :], T8[:, m, :], SM[:, m, :], -3e38)
                    link(ins)
                    link(nc.vector.tensor_tensor(MK, MK, SM, ALU.not_equal))
                    nc.vector.tensor_tensor(WW, SG, MK, ALU.mult).then_inc(mask_ready, 1)
                    dve.wait_ge(mask_ready, 1)
                    link(nc.vector.tensor_reduce(WSUM, WW, AX.X, ALU.add))
                    link(nc.vector.reciprocal(WSUM, WSUM))
                    link(nc.vector.tensor_tensor(WW, WW, WSUM.unsqueeze(2).broadcast_to([P, NT, NE]), ALU.mult))
                    link(nc.vector.tensor_scalar(WW, WW, ROUTED_SCALE, None, ALU.mult))
                elif st == "counts":
                    dve.wait_ge(pos_ready, 1)
                    link(nc.vector.tensor_copy(CNT, PS[:, 7, 0:NE]))
                    link(nc.vector.tensor_scalar(NEX, CNT, 0.0, None, ALU.is_gt))
                    for lim in range(P, T, P):
                        link(nc.vector.tensor_scalar(TMP, CNT, float(lim), None, ALU.is_gt))
                        link(nc.vector.tensor_tensor(NEX, NEX, TMP, ALU.add))
                    link(nc.vector.tensor_tensor_scan(END, ones[:, 0:NE], NEX, 0.0, ALU.mult, ALU.add))
                    link(nc.vector.tensor_tensor(STA, END, NEX, ALU.subtract))
                    link(nc.vector.scalar_tensor_tensor(SE, PS[:, 6, 0:NT * NE].rearrange("p (m e) -> p m e", m=NT), 1.0, MK,
                                                        ALU.add, ALU.mult))
                    link(nc.vector.tensor_scalar(TMP, STA, float(P), -1.0, ALU.mult, ALU.add))
                    link(nc.vector.tensor_tensor(SE, SE, TMP.unsqueeze(1).broadcast_to([P, NT, NE]), ALU.add))
                    rcol = kc(K_COL)[:, 0:1]
                    link(nc.vector.tensor_scalar(EON, STA, rcol, None, ALU.is_le))
                    link(nc.vector.tensor_scalar(TMP, END, rcol, None, ALU.is_gt))
                    link(nc.vector.tensor_tensor(EON, EON, TMP, ALU.mult))
                    link(nc.vector.tensor_tensor(TMP, EON, kc(K_R128)[:, 0:NE], ALU.mult))
                    nc.vector.tensor_reduce(NCNT, TMP, AX.X, ALU.add).then_inc(tab_ready, 1)
                    dve.wait_ge(tab_ready, 1)
                elif st == "table":
                    dve.wait_ge(pr_ready, 1)
                    for m in range(NT):
                        link(nc.vector.scalar_tensor_tensor(POSR[:, m, :], kc(K_R128), -float(P), PS[:, 3, m * P:(m + 1) * P],
                                                            ALU.mult, ALU.add))
                    link(nc.vector.tensor_copy(ROW[0:1, RTAB:RTAB + 1], END[0:1, NE - 1:NE]))
                    nc.vector.tensor_copy(ROW[0:1, 0:RTAB], PS[0:1, 7, 128:256]).then_inc(row_done, 1)
                    for b in range(2):
                        ins = nc.vector.tensor_copy(RHS[:, b, :, 0:3], kc(K_TOK).rearrange("p (m c) -> p m c", m=NT))
                    link(ins)
                    dve.wait_ge(comb_done, 1)
                    link(nc.vector.tensor_copy(OH[:, 0, :, :], COMB))
                    link(nc.vector.tensor_tensor(COMBL, COMB, OH[:, 0, :, :].bitcast(F32), ALU.subtract))
                    one_hots(0, 0)
                    one_hots(1, 1)
                elif st == "index":
                    r = ev[1]
                    take_index(r, r)
                    if r + 2 < AHEAD:
                        one_hots(r + 2, r % 2)
                elif st == "sh_up":
                    m = ev[1]
                    dve.wait_ge(ss_done, m + 1)
                    if m >= 2:
                        dve.wait_ge(sht_ready, m - 1)
                    nc.vector.tensor_tensor(HID[:, m % 2, :], HS[:, m % 2, :], PS[:, 4 + min(m, 1), DE:2 * DE], ALU.mult).then_inc(sh_hid, 1)

            def hidden(r, b):
                dve.wait_ge(silu_done, r + 1)
                nc.vector.tensor_tensor(HID[:, b, :], HS[:, b, :], PS[:, 2 + b, DE:2 * DE], ALU.mult).then_inc(hid_done, 1)

            one_hots(AHEAD, AHEAD % 2)
            take_index(AHEAD, AHEAD)
            hidden(0, 0)
            rounds = dve.value_load(round_count(dve), min_val=1, max_val=ROUNDS)
            with dve.Fori(0, PASSES) as pas:
                with dve.If(pas * BODY + 1 <= rounds):
                    for p in range(BODY):
                        i = pas * BODY + (1 + p)
                        with dve.If(i <= rounds):
                            one_hots(i + AHEAD, (1 + p + AHEAD) % 2)
                            take_index(i + AHEAD, (1 + p + AHEAD) % BODY)
                            dve.wait_ge(ht_ready, i)
                            hidden(i, (1 + p) % 2)
                            dve.wait_ge(dn_ready, i)
                            dve.wait_ge(added, i)
                            nc.vector.tensor_scalar(YS[:, p % 2, :].rearrange("p (a n) -> p a n", a=2), PS[:, 6:8, :],
                                                    WC[:, p:p + 1], None, ALU.mult).then_inc(ys_done, 1)
            def residual(m):
                dve.wait_ge(y_back[m], 16)
                link(nc.vector.tensor_tensor(YF[:, m, :], YF[:, m, :], GBC[:, 1, min(m, 1), :], ALU.mult))
                nc.vector.tensor_tensor(YF[:, m, :], YF[:, m, :], XH[:, m, :], ALU.add).then_inc(h2_done, 1)

            residual(0)
            for m in range(NT):
                if m + 1 < NT:
                    residual(m + 1)
                col = lambda i: small[:, i + m:i + m + 1]
                dve.wait_ge(ssq3, m + 1)
                nc.vector.tensor_scalar(col(4), col(0), 1.0 / D, EPS, ALU.mult, ALU.add).then_inc(ms3, 1)
                dve.wait_ge(ms3, m + 1)
                dve.wait_ge(root3, m + 1)
                rsqrt_fix(col(4), col(8), col(12), col(24))
                nc.vector.scalar_tensor_tensor(YN[:, m, :], YF[:, m, :], col(12), FG, ALU.mult, ALU.mult).then_inc(fin_done, 1)

        @block.tensor
        def _(pe):
            mm = nc.tensor.matmul

            def product(out, lhs, rhs, n):
                for k in range(n):
                    last = mm(out, lhs(k), rhs(k), start=(k == 0), stop=(k == n - 1))
                return last

            def index(r, b):
                pe.wait_ge(oh_done, r + 1)
                if not isinstance(r, int) or r > 0:
                    pe.wait_ge(idx_done, r)
                product(PS[:, 4, 0:4], lambda m: OH[:, b, m, :], lambda m: RHS[:, b, m, :], NT).then_inc(ix_ready, 1)

            for ev in SCHEDULE:
                st = ev[0]
                if st == "norm1":
                    pass
                elif st == "unit":
                    n = ev[1]
                    name, c, j = UNITS[n]
                    if n >= 2:
                        pe.wait_ge(unit_taken, n - 1)
                    bank = n % 2
                    if name == "ada":
                        if c == 0:
                            pe.wait_ge(csil_ready, 1)
                        arrived(pe, ("ada", c))
                        w = slot(("ada", c)).rearrange("p (k n) -> p k n", k=KD)
                        product(PS[0:2, bank, :], lambda k: csil[:, k, :], lambda k: w[:, k, :], KD).then_inc(unit_ready, 1)
                    else:
                        tok = name in TOK_CHUNKS
                        if j == 0:
                            arrived(pe, ("in", c))
                            if c == 0:
                                pe.wait_ge(n_ready, KD)
                        w = slot(("in", c)).rearrange("p (k n) -> p k n", k=KD)
                        if name in SPLIT:
                            _, low, i = half_of(name, j // 2)
                            pe.wait_ge(wlo_done, i + 1)
                            cols, out = slice(j % 2 * P, (j % 2 + 1) * P), PS[:, bank, 0:T]
                            for k in range(KD):
                                if name == SPLIT[0] and j == 0:
                                    pe.wait_ge(nlo_done, k + 1)
                                wh, wl = WHI[:, i % 2, k, cols], low[:, k, cols]
                                nh, nl = NHI[:, k, :], NLO[:, k, :]
                                mm(out, wh, nh, start=(k == 0), stop=False)
                                mm(out, wh, nl, start=False, stop=False)
                                last = mm(out, wl, nh, start=False, stop=(k == KD - 1))
                            last.then_inc(unit_ready, 1)
                            continue
                        if n in SPLIT_G:
                            _, low, i = gate_unit(n)
                            if i == 0:
                                pe.wait_ge(nmove_done, 1)
                            pe.wait_ge(glo_done, i + 1)
                            out = PS[:, bank, 0:T]
                            for k in range(KD):
                                mm(out, GHI[i % 2][:, k, :], NHI2[:, k, :], start=(k == 0), stop=False)
                                mm(out, GHI[i % 2][:, k, :], NLO[:, k, :], start=False, stop=False)
                                last = mm(out, low[:, k, :], NHI2[:, k, :], start=False, stop=(k == KD - 1))
                            last.then_inc(unit_ready, 1)
                        elif n == SPLIT_G[-1] + 1:
                            cols = slice(j * P, (j + 1) * P)
                            for k in range(KD):
                                pe.wait_ge(nback_done, k + 1)
                                last = mm(PS[:, bank, 0:T], w[:, k, cols], nT[:, k, :], start=(k == 0), stop=(k == KD - 1))
                            last.then_inc(unit_ready, 1)
                        elif tok:
                            product(PS[:, bank, :], lambda k: nT[:, k, j * P:(j + 1) * P], lambda k: w[:, k, :], KD).then_inc(unit_ready, 1)
                        else:
                            product(PS[:, bank, 0:T], lambda k: w[:, k, j * P:(j + 1) * P], lambda k: nT[:, k, :], KD).then_inc(unit_ready, 1)
                elif st == "mod1":
                    pe.wait_ge(unit_taken, 4)
                    pe.wait_ge(in_small, 16)
                    for s in range(2):
                        for k in range(KD):
                            last = mm(PS[:, 7, (s * KD + k) * 2:(s * KD + k) * 2 + 2], ADA[0:2, s * D + k:(s + 1) * D:KD],
                                      ident[0:2, 0:2], start=True, stop=True)
                    last.then_inc(modt_ready, 1)
                    pe.wait_ge(xn_ready, NT)
                    for k in range(KD):
                        if k >= 4:
                            pe.wait_ge(n_ready, k - 3)
                        for m in range(NT):
                            last = nc.tensor.transpose(PS[:, 2 + k % 4, m * P:(m + 1) * P], XN[:, m, k:D:KD], ident)
                        last.then_inc(xnt_ready, 1)
                elif st == "cache":
                    pe.wait_ge(in_cache, 32)
                    for j in range(4):
                        last = nc.tensor.transpose(PS[:, 4, j * P:(j + 1) * P], CK[:, j * P:(j + 1) * P], ident)
                    last.then_inc(ck_t, 1)
                    pe.wait_ge(unit_taken, AFTER["k"])
                    for j in range(4):
                        last = nc.tensor.transpose(PS[:, 5, j * P:(j + 1) * P], KT[:, j, 0:CTX], ident)
                    last.then_inc(ck_t, 1)
                elif st == "scores":
                    h = ev[1]
                    o, j = 64 * (h % 2), h // 2
                    pe.wait_ge(unit_taken, AFTER["k"])
                    pe.wait_ge(ck_taken, 2)
                    for u in range(3):
                        i = 3 * h + u
                        if i >= 2:
                            pe.wait_ge(s_taken, i - 1)
                        bank = 2 + i % 2
                        if u < 2:
                            q = Q[o:o + DH, j, CTX + u * P:CTX + (u + 1) * P]
                            mm(PS[:, bank, 0:2 * P], q, KT[o:o + DH, j, CTX:T], start=True, stop=True)
                            mm(PS[:, bank, 2 * P:3 * P], q, CKT[o:o + DH, j, :], start=True, stop=True).then_inc(s_ready, 1)
                        else:
                            mm(PS[:, bank, 0:P], Q[o:o + DH, j, 0:CTX], KT[o:o + DH, j, 0:CTX], start=True, stop=True).then_inc(s_ready, 1)
                elif st == "values":
                    h = ev[1]
                    o = 64 * (h % 2)
                    for u in range(3):
                        i = 3 * h + u
                        pe.wait_ge(prob_ready, i + 1)
                        if i > 0:
                            pe.wait_ge(pt_taken, i)
                        nk = 3 if u < 2 else 1
                        for k in range(nk):
                            last = nc.tensor.transpose(PS[:, 4, k * P:(k + 1) * P], PR[:, u, k * P:(k + 1) * P], ident)
                        last.then_inc(pt_ready, 1)
                    if h > 0:
                        pe.wait_ge(pv_taken, h)
                    pe.wait_ge(pt_taken, 3 * h + 3)
                    vs = [V[:, 1, h * DH:(h + 1) * DH], V[:, 2, h * DH:(h + 1) * DH], CV[:, h * DH:(h + 1) * DH]]
                    product(PS[o:o + DH, 5, 0:2 * P], lambda k: vs[k], lambda k: PT[:, k, :], 3)
                    mm(PS[o:o + DH, 5, 2 * P:3 * P], V[:, 0, h * DH:(h + 1) * DH], PTC, start=True, stop=True).then_inc(pv_ready, 1)
                elif st == "level":
                    i = ev[1]
                    pe.wait_ge(qk_done, i + 1)
                    if i > 0:
                        pe.wait_ge(lev_taken, i)
                    for hh in range(2):
                        for m in range(NT):
                            s = slice(hh * T + m * P, hh * T + (m + 1) * P)
                            last = mm(PS[:, 6 + hh, m * P:(m + 1) * P], KX[:, s], QX[:, s], start=True, stop=True)
                    last.then_inc(lev_ready, 1)
                elif st == "carry_t":
                    for c in range(4):
                        pe.wait_ge(kh_done, c + 1)
                        if c >= 2:
                            pe.wait_ge(kht_taken, c - 1)
                        for h in range(HC):
                            last = nc.tensor.transpose(PS[:, 4 + c % 2, h * P:(h + 1) * P], KH[:, c, h, :], ident)
                        last.then_inc(kht_ready, 1)
                elif st == "carry_products":
                    pe.wait_ge(lev_taken, 16)
                    pe.wait_ge(unit_taken, AFTER["ic"])
                    for c, m in enumerate((0, 0, 1, 2)):
                        pe.wait_ge(kht_taken, c + 1)
                        if c == 2:
                            pe.wait_ge(st_done, 1)
                        if c == 3:
                            pe.wait_ge(st_done, 2)
                        for h in range(HC):
                            last = mm(PS[:, 6 + c % 2, h * P:(h + 1) * P], KHT[:, c, h, :], IC[:, m, h * P:(h + 1) * P], start=True, stop=True)
                        last.then_inc(kv_ready, 1)
                elif st == "hout":
                    m = ev[1]
                    if m == 0:
                        pe.wait_ge(st_done, 3)
                    else:
                        pe.wait_ge(ho_taken, m)
                    for h in range(HC):
                        out = PS[:, 6, h * P:(h + 1) * P]
                        v = IC[:, m, h * P:(h + 1) * P]
                        last = mm(out, AT_[:, h, m, :], v, start=True, stop=(m == 0))
                        if m > 0:
                            sf = ST if m == 1 else ST2
                            sb_ = ST if m == 2 else ST2
                            mm(out, EB[:, 0, h, (m - 1) * P:m * P], sf[:, 0, h, :], start=False, stop=False)
                            last = mm(out, EB[:, 1, h, (m - 1) * P:m * P], sb_[:, 1, h, :], start=False, stop=True)
                    last.then_inc(ho_ready, 1)
                elif st == "hout_t":
                    m = ev[1]
                    pe.wait_ge(ho_norm, m + 1)
                    if m > 0:
                        pe.wait_ge(hot_taken, m)
                    for h in range(HC):
                        last = nc.tensor.transpose(PS[:, 7, h * P:(h + 1) * P], OR[:, h * P:(h + 1) * P], ident)
                    last.then_inc(hot_ready, 1)
                elif st == "mod2":
                    for s in range(2):
                        for k in range(KD):
                            last = mm(PS[:, 7, (s * KD + k) * 2:(s * KD + k) * 2 + 2], Zrows[:, s * D + k:(s + 1) * D:KD],
                                      ident[0:2, 0:2], start=True, stop=True)
                    last.then_inc(modt_ready, 1)
                elif st == "gate1":
                    pe.wait_ge(gr_ready, 1)
                    pe.wait_ge(br_taken, 24)
                    for i in range(4):
                        mm(PS[:, 2 + i, :], sel[0:2, i // 2, :], GR[0:2, i % 2 * 512:(i % 2 + 1) * 512],
                           start=True, stop=True).then_inc(gb_ready, 1)
                elif st == "gate2":
                    for i in range(4):
                        pe.wait_ge(gb_taken, i + 1)
                        mm(PS[:, 2 + i, :], sel[0:2, i // 2, :], GR[0:2, D + i % 2 * 512:D + (i % 2 + 1) * 512],
                           start=True, stop=True).then_inc(g2_ready, 1)
                elif st == "branches":
                    pe.wait_ge(unit_taken, len(UNITS))
                    pe.wait_ge(hot_taken, NT)
                    for i in range(24):
                        br, j = i // KD, i % KD
                        if j == 0:
                            arrived(pe, ("br", br))
                        if i >= 6:
                            pe.wait_ge(br_taken, i - 5)
                        w = slot(("br", br)).rearrange("p (k n) -> p k n", k=4)
                        src = (OA, GB, OCT)[br]
                        product(PS[:, i % 6, 0:T], lambda k: w[:, k, j * P:(j + 1) * P], lambda k: src[:, k, :], 4).then_inc(br_ready, 1)
                elif st == "wout":
                    m, hf = ev[1:]
                    pe.wait_ge(mix_done, 2 * KD)
                    pe.wait_ge(mod_ready, 2)
                    arrived(pe, ("out", hf))
                    if m > 0:
                        pe.wait_ge(wo_taken, 2 * m + hf - 1)
                    w = slot(("out", hf)).rearrange("p (k n) -> p k n", k=KD)
                    product(PS[:, 6 + hf, :], lambda k: G[:, k, m * P:(m + 1) * P], lambda k: w[:, k, :], KD).then_inc(wo_ready, 1)
                elif st == "norm_t":
                    m = ev[1]
                    pe.wait_ge(xn2, m + 1)
                    if m > 0:
                        pe.wait_ge(n2_ready, m)
                    for k in range(KD):
                        last = nc.tensor.transpose(PS[:, k // 4, k % 4 * P:(k % 4 + 1) * P], XN2[:, m, k:D:KD], ident)
                    last.then_inc(xnt2, 1)
                elif st == "rows":
                    m = ev[1]
                    pe.wait_ge(n2_ready, m + 1)
                    if m == 0:
                        pe.wait_ge(g2_taken, 4)
                    for hf in range(2):
                        if m > 0:
                            pe.wait_ge(n2_rowed, 2 * m + hf - 1)
                        for k in range(4):
                            last = nc.tensor.transpose(PS[:, 2 + hf, k * P:(k + 1) * P], nT[:, 4 * hf + k, m * P:(m + 1) * P], ident)
                        last.then_inc(n2t_ready, 1)
                elif st == "router":
                    pe.wait_ge(fin_loaded, 48)
                    pe.wait_ge(wo_taken, 2 * NT)
                    pe.wait_ge(n2_ready, NT)
                    for m in range(NT):
                        last = product(PS[:, 6, m * NE:(m + 1) * NE], lambda k: nT[:, k, m * P:(m + 1) * P], lambda k: WR[:, k, :], KD)
                    last.then_inc(rt_ready, 1)
                elif st == "counts":
                    pe.wait_ge(mask_ready, 1)
                    for m in range(NT):
                        lhs = [ones] * m + [kc(K_TRI)]
                        last = product(PS[:, 6, m * NE:(m + 1) * NE], lambda k: lhs[k], lambda k: MK[:, k, :], m + 1)
                    product(PS[:, 7, 0:NE], lambda k: ones, lambda k: MK[:, k, :], NT).then_inc(pos_ready, 1)
                elif st == "table_t":
                    pe.wait_ge(tab_ready, 1)
                    nc.tensor.transpose(PS[0:NE, 6, 0:P], EON, ident)
                    for m in range(NT):
                        nc.tensor.transpose(PS[0:NE, 6, (m + 1) * P:(m + 2) * P], SE[:, m, :], ident)
                        last = nc.tensor.transpose(PS[0:NE, 7, m * P:(m + 1) * P], WW[:, m, :], ident)
                    last.then_inc(te_ready, 1)
                elif st == "table":
                    pe.wait_ge(te_taken, 1)
                    pe.wait_ge(n2_rowed, 2 * NT)
                    mm(PS[0:1, 7, P:2 * P], NCNT, ident, start=True, stop=True)
                    for m in range(NT):
                        mm(PS[:, 3, m * P:(m + 1) * P], TE[0:NE, 1 + m, :], TE[0:NE, 0, :], start=True, stop=True)
                        last = mm(PS[:, 6, m * P:(m + 1) * P], TE[0:NE, 4 + m, :], TE[0:NE, 0, :], start=True, stop=True)
                    last.then_inc(pr_ready, 1)
                elif st == "sh_up":
                    m = ev[1]
                    if m == 0:
                        pe.wait_ge(sh_loaded, 48)
                        pe.wait_ge(g2_taken, 4)
                    wg = slot(("sh", 0)).rearrange("p (k n) -> p k n", k=KD)
                    if m >= 2:
                        pe.wait_ge(sh_hid, m)
                    product(PS[:, 4 + min(m, 1), :], lambda k: nT[:, k, m * P:(m + 1) * P], lambda k: wg[:, k, :], KD).then_inc(sg_ready, 1)
                elif st == "index":
                    if ev[1] == 0:
                        pe.wait_ge(sh_hid, 1)
                    index(ev[1], ev[1] % 2)
                elif st == "sh_down":
                    m = ev[1]
                    wd = slot(("shd", 0))[:, 0:2 * D].rearrange("p (k n) -> p k n", k=2)
                    pe.wait_ge(n2_ready, NT)
                    pe.wait_ge(n2_rowed, 2 * NT)
                    pe.wait_ge(sh_hid, m + 1)
                    if m > 0:
                        pe.wait_ge(sht_taken, m)
                    for k in range(2):
                        last = nc.tensor.transpose(PS[:, 0, k * P:(k + 1) * P], HID[:, m % 2, k * P:(k + 1) * P], ident)
                    last.then_inc(sht_ready, 1)
                    pe.wait_ge(sht_taken, m + 1)
                    if m > 0:
                        pe.wait_ge(sho_done, m)
                    for hf in range(2):
                        last = product(PS[:, 1 + hf, :], lambda k: HT[:, m % 2, k, :], lambda k: wd[:, k, hf * 512:(hf + 1) * 512], 2)
                    last.then_inc(shd_ready, 1)

            def transposes(turn, b):
                pe.wait_ge(gathered[b], 16 * turn)
                for k in range(KD):
                    last = nc.tensor.transpose(PS[:, k // 4, k % 4 * P:(k % 4 + 1) * P], XG[:, b, k:D:KD], ident)
                last.then_inc(xg_t, 1)

            def gate_up(r, turn, p, ks):
                b, q = p % 2, p % WS
                if 0 in ks:
                    pe.wait_ge(gu_loaded[q], 32 * turn)
                    pe.wait_ge(xt_done, r + 1)
                for k in ks:
                    last = mm(PS[:, 2 + b, :], XT[:, b, k, :], GU_W[q][:, k, :], start=(k == 0), stop=(k == KD - 1))
                if KD - 1 in ks:
                    last.then_inc(gu_ready, 1)

            pe.wait_ge(sho_done, NT)
            transposes(1, 0)
            pe.wait_ge(xt_done, 1)
            transposes(1, 1)
            index(AHEAD, AHEAD % 2)
            gate_up(0, 1, 0, range(KD))
            rounds = pe.value_load(round_count(pe), min_val=1, max_val=ROUNDS)
            with pe.Fori(0, PASSES) as pas:
                with pe.If(pas * BODY + 1 <= rounds):
                    for p in range(BODY):
                        i = pas * BODY + (1 + p)
                        with pe.If(i <= rounds):
                            pe.wait_ge(xt_done, i + 1)
                            transposes(pas * (BODY // XGS) + (2 + p) // XGS + 1, (2 + p) % XGS)
                            pe.wait_ge(hid_done, i)
                            turn = pas * (BODY // WS) + (1 + p) // WS + 1
                            gate_up(i, turn, 1 + p, range(0, 4))
                            pe.wait_ge(hid_done, i + 1)
                            for k in range(2):
                                last = nc.tensor.transpose(PS[:, 5, k * P:(k + 1) * P], HID[:, p % 2, k * P:(k + 1) * P], ident)
                            last.then_inc(ht_ready, 1)
                            index(i + AHEAD, (1 + p + AHEAD) % 2)
                            gate_up(i, turn, 1 + p, range(4, KD))
                            q = p % WS
                            pe.wait_ge(dn_loaded[q], 16 * (pas * (BODY // WS) + p // WS + 1))
                            pe.wait_ge(ht_done, i)
                            pe.wait_ge(ys_done, i)
                            for hf in range(2):
                                last = product(PS[:, 6 + hf, :], lambda k: HT[:, p % 2, k, :],
                                               lambda k: DN_W[q][:, k, hf * 512:(hf + 1) * 512], 2)
                            last.then_inc(dn_ready, 1)


_OUTS = [("y", (T, D)), ("new_k", (P, 512)), ("new_v", (P, 512)), ("new_state", (2, HC, P, P))]


def kernel(**inputs):
    import concourse.bacc as _bacc
    from concourse.bass_utils import run_bass_kernel_spmd as _run

    a = {k: np.ascontiguousarray(v) for k, v in inputs.items()}
    pk = lambda v: v.reshape(P, KD)
    hp = lambda v: v.reshape(-1, P).T
    b_ada = a["b_ada"][0].reshape(6, D)
    cols = np.concatenate(
        [pk(a["norm1_g"][0]), pk(a["norm2_g"][0]), pk(a["c_ctx"]), pk(a["c"][0])]
        + [pk(b_ada[i]) for i in (0, 1, 3, 4)]
        + [hp(a["lb_fwd"][0]), hp(a["lb_bwd"][0]), hp(a["w_conv"][0]), hp(a["hgrn_norm_g"][0])], 1)
    w_ada = a["w_ada"][0]
    arrays = {
        "x": np.concatenate([a["x_prompt"][0], a["x_sample"][0]], 0),
        "consts": shape_constants(),
        "cols": cols,
        "b_gate": np.tile(np.concatenate([b_ada[2], b_ada[5]])[None], (2, 1)),
        "w_ada": w_ada,
        "w_in": a["w_in"][0],
        "w_br": np.concatenate([a["w_br_a"], a["w_br_b"], a["w_br_c"]], 0),
        "w_out": a["w_out"][0],
        "rpb": a["rpb"][0],
        "cache_k": a["cache_k"].reshape(P, 512),
        "cache_v": a["cache_v"].reshape(P, 512),
        "state": a["state_hgrn"][0, 0],
        "w_router": a["w_router"][0],
        "b_router": a["b_router"][0],
        "w_sh_gate": a["w_sh_gate"][0],
        "w_sh_up": a["w_sh_up"][0],
        "w_sh_down": a["w_sh_down"][0],
        "w_gate": a["w_gate"][0],
        "w_up": a["w_up"][0],
        "w_down": a["w_down"][0],
        "final_g": a["final_norm_g"],
    }
    arrays = {k: np.ascontiguousarray(v) for k, v in arrays.items()}
    nc = _bacc.Bacc("TRN2", target_bir_lowering=False, num_devices=1)
    args = [nc.dram_tensor(f"in_{k}", v.shape, mybir.dt.from_np(v.dtype), kind="ExternalInput").ap() for k, v in arrays.items()]
    outs = [nc.dram_tensor(f"out_{k}", shape, F32, kind="ExternalOutput").ap() for k, shape in _OUTS]
    trunk(nc, *args, *outs)
    r = _run(nc, [{f"in_{k}": v for k, v in arrays.items()}], core_ids=[0]).results[0]
    y = r["out_y"]
    return (y[:P].reshape(1, P, D), y[P:].reshape(1, T - P, D),
            r["out_new_k"].reshape(1, 1, P, NH, DH), r["out_new_v"].reshape(1, 1, P, NH, DH),
            r["out_new_state"].reshape(1, 1, 2, HC, P, P))
```
